# Optimizing a Trainium2 kernel written in Bass

```python
import jax, jax.numpy as jnp
from jax import lax
import numpy as np

D_MODEL = 1024
BATCH = 1
SEQ = 512
DEPTH = 2
DEC_BATCH = 8
DEC_SEQ = 1
PAST_LEN = 2048
PAGE_SIZE = 128

N_HEADS = 8
N_KV_HEADS = 2
KV_GROUP = N_HEADS // N_KV_HEADS
ATTN_WIDTH = D_MODEL // 2
HEAD_DIM = ATTN_WIDTH // N_HEADS
ROPE_THETA = 500000.0
N_IDX_HEADS = 8
IDX_DIM = 64
TOPK_MAX = 256
Q_BLOCK = 128
POOL_WINDOWS = (2, 4, 8, 16)
N_POOL_GROUPS = len(POOL_WINDOWS)
POOL_WIDTH = D_MODEL - ATTN_WIDTH
POOL_GROUP_DIM = POOL_WIDTH // N_POOL_GROUPS
POOL_BUF = max(POOL_WINDOWS) - 1
D_FF = 2816
CONV_WIDTH = 3
RMS_EPS = 1e-6
SPLIT_SIZES = (ATTN_WIDTH, N_KV_HEADS * HEAD_DIM, N_KV_HEADS * HEAD_DIM,
               N_IDX_HEADS * IDX_DIM, IDX_DIM, N_IDX_HEADS, POOL_WIDTH)
IN_WIDTH = sum(SPLIT_SIZES)

kernel_name = "hymba_dsa_pool_convffn_step"

def rms_norm(x, g):
    xf = x.astype(jnp.float32)
    y = xf * lax.rsqrt(jnp.mean(xf * xf, axis=-1, keepdims=True) + RMS_EPS)
    return (y * g.astype(jnp.float32)).astype(x.dtype)

def partial_rope(x, pos):
    rot = x.shape[-1] // 4
    half = rot // 2
    inv = ROPE_THETA ** (-jnp.arange(half, dtype=jnp.float32) / half)
    ang = pos.astype(jnp.float32)[:, None] * inv[None, :]
    cos = jnp.cos(ang)[None, :, None, :]
    sin = jnp.sin(ang)[None, :, None, :]
    xr = x[..., :rot].astype(jnp.float32)
    x1, x2 = xr[..., :half], xr[..., half:]
    r = jnp.concatenate([x1 * cos - x2 * sin, x2 * cos + x1 * sin], axis=-1).astype(x.dtype)
    return jnp.concatenate([r, x[..., rot:]], axis=-1)

def project(h, w_in, pos):
    B, T = h.shape[:2]
    z = h @ w_in
    cuts = [int(c) for c in np.cumsum(SPLIT_SIZES)[:-1]]
    q, k, v, qi, ki, wi, xp = jnp.split(z, cuts, axis=-1)
    q = partial_rope(q.reshape(B, T, N_HEADS, HEAD_DIM), pos)
    k = partial_rope(k.reshape(B, T, N_KV_HEADS, HEAD_DIM), pos)
    v = v.reshape(B, T, N_KV_HEADS, HEAD_DIM)
    qi = partial_rope(qi.reshape(B, T, N_IDX_HEADS, IDX_DIM), pos)
    ki = partial_rope(ki.reshape(B, T, 1, IDX_DIM), pos)[:, :, 0]
    return q, k, v, qi, ki, wi, xp

def indexer_scores(qi, wi, ki, q_pos, k_pos):
    dots = jnp.einsum('bqhd,bld->bqhl', qi, ki) * (IDX_DIM ** -0.5)
    s = jnp.einsum('bqhl,bqh->bql', jax.nn.relu(dots), wi).astype(jnp.float32) * (N_IDX_HEADS ** -0.5)
    return jnp.where(k_pos[None, None, :] <= q_pos[None, :, None], s, -jnp.inf)

def sparse_attend(q, k_sel, v_sel, valid):
    B, Q = q.shape[:2]
    qg = q.reshape(B, Q, N_KV_HEADS, KV_GROUP, HEAD_DIM)
    s = jnp.einsum('bqngd,bqknd->bqngk', qg, k_sel).astype(jnp.float32) * (HEAD_DIM ** -0.5)
    s = jnp.where(valid[:, :, None, None, :], s, -jnp.inf)
    p = jax.nn.softmax(s, axis=-1).astype(v_sel.dtype)
    o = jnp.einsum('bqngk,bqknd->bqngd', p, v_sel)
    return o.reshape(B, Q, ATTN_WIDTH)

def prompt_attention(q, k, v, qi, ki, wi):
    B, S = q.shape[:2]
    topk = min(TOPK_MAX, S // 4)
    k_pos = jnp.arange(S)
    bidx = jnp.arange(B)[:, None, None]

    def block(i):
        q0 = i * Q_BLOCK
        qb = lax.dynamic_slice_in_dim(q, q0, Q_BLOCK, axis=1)
        qib = lax.dynamic_slice_in_dim(qi, q0, Q_BLOCK, axis=1)
        wib = lax.dynamic_slice_in_dim(wi, q0, Q_BLOCK, axis=1)
        q_pos = q0 + jnp.arange(Q_BLOCK)
        sc = indexer_scores(qib, wib, ki, q_pos, k_pos)
        _, sel = lax.top_k(sc, topk)
        valid = sel <= q_pos[None, :, None]
        return sparse_attend(qb, k[bidx, sel], v[bidx, sel], valid)

    out = lax.map(block, jnp.arange(S // Q_BLOCK))
    return out.transpose(1, 0, 2, 3).reshape(B, S, ATTN_WIDTH)

def sample_attention(q, k_new, v_new, qi, ki_new, wi, ck, cv, cki, page_table):
    B, T = q.shape[:2]
    past = page_table.shape[1] * PAGE_SIZE
    L = past + T
    topk = min(TOPK_MAX, L // 4)
    ki_past = cki[page_table].reshape(B, past, IDX_DIM)
    ki_all = jnp.concatenate([ki_past, ki_new], axis=1)
    q_pos = past + jnp.arange(T)
    sc = indexer_scores(qi, wi, ki_all, q_pos, jnp.arange(L))
    _, sel = lax.top_k(sc, topk)
    valid = sel <= q_pos[None, :, None]
    bidx = jnp.arange(B)[:, None, None]
    in_past = (sel < past)[..., None, None]
    sp = jnp.minimum(sel, past - 1)
    phys = page_table[bidx, sp // PAGE_SIZE]
    off = sp % PAGE_SIZE
    sn = jnp.clip(sel - past, 0, T - 1)
    k_sel = jnp.where(in_past, ck[phys, off], k_new[bidx, sn])
    v_sel = jnp.where(in_past, cv[phys, off], v_new[bidx, sn])
    return sparse_attend(q, k_sel, v_sel, valid)

def pool_mixer(x_ext, n_out, w_pool, pool_scale):
    B, R = x_ext.shape[:2]
    xg = x_ext.reshape(B, R, N_POOL_GROUPS, POOL_GROUP_DIM).astype(jnp.float32)
    cs0 = jnp.concatenate([jnp.zeros_like(xg[:, :1]), jnp.cumsum(xg, axis=1)], axis=1)
    idx = jnp.arange(R - n_out, R)
    win = jnp.asarray(POOL_WINDOWS, jnp.int32)
    lo = jnp.maximum(idx[:, None] + 1 - win[None, :], 0)
    gidx = jnp.arange(N_POOL_GROUPS)[None, :]
    wsum = cs0[:, idx + 1] - cs0[:, lo, gidx]
    count = (idx[:, None] + 1 - lo).astype(jnp.float32)
    diff = (wsum / count[None, :, :, None] - xg[:, R - n_out:]).astype(x_ext.dtype)
    out = jnp.einsum('btgc,gcd->btgd', diff, w_pool).reshape(B, n_out, POOL_WIDTH)
    return out * pool_scale

def conv_ffn(h, buf, w_gate, w_val, conv_w, conv_b, w_down):
    g = h @ w_gate
    T = g.shape[1]
    ext = jnp.concatenate([buf, g], axis=1)
    c = conv_b + sum(ext[:, j:j + T] * conv_w[j] for j in range(CONV_WIDTH))
    y = (jax.nn.gelu(c, approximate=True) * (h @ w_val)) @ w_down
    return y, ext[:, -(CONV_WIDTH - 1):]

def layer(x, pos, attn_fn, pool_prev, conv_prev, p):
    T = x.shape[1]
    h = rms_norm(x, p['g_pre_mix'])
    q, k, v, qi, ki, wi, xp = project(h, p['w_in'], pos)
    a = attn_fn(q, k, v, qi, ki, wi)
    pool_ext = jnp.concatenate([pool_prev, xp], axis=1)
    m = pool_mixer(pool_ext, T, p['w_pool'], p['pool_scale'])
    mix = jnp.concatenate([a, m], axis=-1) @ p['w_out']
    x = x + rms_norm(mix, p['g_post_mix'])
    h2 = rms_norm(x, p['g_pre_ffn'])
    f, conv_new = conv_ffn(h2, conv_prev, p['w_gate'], p['w_val'], p['conv_w'], p['conv_b'], p['w_down'])
    x = x + rms_norm(f, p['g_post_ffn'])
    return x, k, v, ki, pool_ext[:, -POOL_BUF:], conv_new

def setup_inputs(seed: int = 0) -> dict:
    key = jax.random.key(seed)
    ks = jax.random.split(key, 24)
    n_pages = PAST_LEN // PAGE_SIZE
    n_phys = (DEC_BATCH * n_pages * 5) // 4
    f32 = jnp.float32
    nrm = lambda k, shape, s=1.0: jax.random.normal(k, shape, f32) * s
    gain = lambda k: 1.0 + 0.05 * jax.random.normal(k, (DEPTH, D_MODEL), f32)
    page_table = jax.random.permutation(ks[7], n_phys)[:DEC_BATCH * n_pages].reshape(DEC_BATCH, n_pages).astype(jnp.int32)
    return {
        'x_prompt': nrm(ks[0], (BATCH, SEQ, D_MODEL)),
        'x_sample': nrm(ks[1], (DEC_BATCH, DEC_SEQ, D_MODEL)),
        'cache_k': nrm(ks[2], (DEPTH, n_phys, PAGE_SIZE, N_KV_HEADS, HEAD_DIM)),
        'cache_v': nrm(ks[3], (DEPTH, n_phys, PAGE_SIZE, N_KV_HEADS, HEAD_DIM)),
        'cache_idx_k': nrm(ks[4], (DEPTH, n_phys, PAGE_SIZE, IDX_DIM)),
        'state_pool': nrm(ks[5], (DEPTH, DEC_BATCH, POOL_BUF, POOL_WIDTH)),
        'state_conv': nrm(ks[6], (DEPTH, DEC_BATCH, CONV_WIDTH - 1, D_FF)),
        'page_table': page_table,
        'g_pre_mix': gain(ks[8]),
        'w_in': nrm(ks[9], (DEPTH, D_MODEL, IN_WIDTH), D_MODEL ** -0.5),
        'w_pool': nrm(ks[10], (DEPTH, N_POOL_GROUPS, POOL_GROUP_DIM, POOL_GROUP_DIM), POOL_GROUP_DIM ** -0.5),
        'pool_scale': 1.0 + 0.1 * nrm(ks[11], (DEPTH, POOL_WIDTH)),
        'w_out': nrm(ks[12], (DEPTH, D_MODEL, D_MODEL), D_MODEL ** -0.5),
        'g_post_mix': gain(ks[13]),
        'g_pre_ffn': gain(ks[14]),
        'w_gate': nrm(ks[15], (DEPTH, D_MODEL, D_FF), D_MODEL ** -0.5),
        'w_val': nrm(ks[16], (DEPTH, D_MODEL, D_FF), D_MODEL ** -0.5),
        'conv_w': nrm(ks[17], (DEPTH, CONV_WIDTH, D_FF), 0.5),
        'conv_b': nrm(ks[18], (DEPTH, D_FF), 0.02),
        'w_down': nrm(ks[19], (DEPTH, D_FF, D_MODEL), D_FF ** -0.5),
        'g_post_ffn': gain(ks[20]),
    }

def reference(x_prompt, x_sample, cache_k, cache_v, cache_idx_k, state_pool, state_conv, page_table,
              g_pre_mix, w_in, w_pool, pool_scale, w_out, g_post_mix, g_pre_ffn,
              w_gate, w_val, conv_w, conv_b, w_down, g_post_ffn):
    Bp, Sp = x_prompt.shape[:2]
    Ts = x_sample.shape[1]
    past = page_table.shape[1] * PAGE_SIZE
    pos_p = jnp.arange(Sp)
    pos_s = past + jnp.arange(Ts)
    yp, ys = x_prompt, x_sample
    kp_l, vp_l, ikp_l, plp_l, cvp_l = [], [], [], [], []
    ks_l, vs_l, iks_l, pls_l, cvs_l = [], [], [], [], []
    for l in range(DEPTH):
        p = dict(g_pre_mix=g_pre_mix[l], w_in=w_in[l], w_pool=w_pool[l], pool_scale=pool_scale[l],
                 w_out=w_out[l], g_post_mix=g_post_mix[l], g_pre_ffn=g_pre_ffn[l], w_gate=w_gate[l],
                 w_val=w_val[l], conv_w=conv_w[l], conv_b=conv_b[l], w_down=w_down[l],
                 g_post_ffn=g_post_ffn[l])
        pool0 = jnp.zeros((Bp, 0, POOL_WIDTH), yp.dtype)
        conv0 = jnp.zeros((Bp, CONV_WIDTH - 1, D_FF), yp.dtype)
        yp, k1, v1, ik1, pl1, cv1 = layer(yp, pos_p, prompt_attention, pool0, conv0, p)
        kp_l.append(k1); vp_l.append(v1); ikp_l.append(ik1); plp_l.append(pl1); cvp_l.append(cv1)
        ck, cv, cki = cache_k[l], cache_v[l], cache_idx_k[l]
        attn_s = lambda q, k, v, qi, ki, wi, ck=ck, cv=cv, cki=cki: sample_attention(
            q, k, v, qi, ki, wi, ck, cv, cki, page_table)
        ys, k2, v2, ik2, pl2, cv2 = layer(ys, pos_s, attn_s, state_pool[l], state_conv[l], p)
        ks_l.append(k2); vs_l.append(v2); iks_l.append(ik2); pls_l.append(pl2); cvs_l.append(cv2)
    return (yp, ys,
            jnp.stack(kp_l), jnp.stack(vp_l), jnp.stack(ikp_l), jnp.stack(plp_l), jnp.stack(cvp_l),
            jnp.stack(ks_l), jnp.stack(vs_l), jnp.stack(iks_l), jnp.stack(pls_l), jnp.stack(cvs_l))


_drawn_inputs = setup_inputs


def setup_inputs(seed=0):
    import zlib

    import numpy as np

    out = dict(_drawn_inputs(seed))
    spreads = {}
    factors = {'conv_b': 2.801}
    for name, (base, spread) in spreads.items():
        noise = np.random.default_rng([zlib.crc32(name.encode()), seed]).standard_normal(out[name].shape)
        drawn = base * np.exp(spread * noise) if base else spread * noise
        out[name] = __import__('jax').numpy.asarray(drawn.astype(out[name].dtype))
    for name, factor in factors.items():
        out[name] = (out[name] * factor).astype(out[name].dtype)
    return out
```

```python
from contextlib import ExitStack

import numpy as np

import concourse.bass as bass
from concourse import mybir

F32 = mybir.dt.float32
BF16 = mybir.dt.bfloat16
I32 = mybir.dt.int32
ALU = mybir.AluOpType
ACT = mybir.ActivationFunctionType
AX = mybir.AxisListType

P = 128
D_MODEL, SEQ, DEPTH, NB = 1024, 512, 2, 8
PAST, PAGE = 2048, 128
N_PHYS = 160
N_HEADS, HD = 8, 64
TOPK_P, TOPK_S = 128, 256
WINDOWS = (2, 4, 8, 16)
POOL_BUF = 15
D_FF = 2816
EPS = 1e-6
ROPE_THETA = 500000.0
Q0, K0, V0, QI0, KI0, XP0, IN_WIDTH = 0, 512, 640, 768, 1280, 1352, 1864

KD = D_MODEL // P
NF = D_FF // P
TOK = SEQ + NB
HT = TOK // 2
NT = SEQ // P
NPG = PAST // PAGE
NPP = NPG // 2
KVW = 328
NEG = -3.0e38
TAKEN = -3.3e38
KEYS_BEFORE = {1: 0, 2: 256, 3: 640}
KEYS_ALL = 1152

_CONST = [("ident", P), ("ones", P), ("cosT", TOK), ("sinT", TOK), ("cosN", 40), ("sinN", 40), ("rot", P),
          ("swap", P), ("mask", 896), ("same", 64), ("below", 64), ("newneg", 1), ("newrow", 64),
          ("newto", 64), ("diag", 8), ("iota16", 16), ("tok", 1), ("row64", 1), ("edge", 60), ("wsel", 32),
          ("bits", 32)]
CO, _n = {}, 0
for _name, _w in _CONST:
    CO[_name] = (_n, _n + _w)
    _n += _w
NCONST = _n


def constants():
    c = np.zeros((P, NCONST), np.float32)

    def put(name, a, rows=P):
        lo, hi = CO[name]
        c[:rows, lo:hi] = a

    put("ident", np.eye(P))
    put("ones", 1.0)
    pos = np.concatenate([np.arange(SEQ), np.full(NB, PAST)]).astype(np.float32)
    half = 8
    inv = (np.float32(ROPE_THETA) ** (-np.arange(half, dtype=np.float32) / np.float32(half))).astype(np.float32)
    ang = (pos[:, None] * inv[None, :]).astype(np.float32).astype(np.float64)
    cos, sin = np.cos(ang), np.sin(ang)
    ct, st, rot = np.ones((P, TOK)), np.zeros((P, TOK)), np.zeros((P, P))
    for p in range(P):
        d = p % HD
        if d < half:
            ct[p], st[p], rot[p + half, p] = cos[:, d], -sin[:, d], 1.0
        elif d < 2 * half:
            ct[p], st[p], rot[p - half, p] = cos[:, d - half], sin[:, d - half], 1.0
    put("cosT", ct * HD ** -0.5)
    put("sinT", st * HD ** -0.5)
    put("rot", rot)
    cn, sn = np.ones((P, 5, half)), np.zeros((P, 5, half))
    for t in range(5):
        rows = P if t < 4 else NB
        cn[:rows, t], sn[:rows, t] = cos[t * P:t * P + rows], sin[t * P:t * P + rows]
    put("cosN", cn.reshape(P, 40))
    put("sinN", sn.reshape(P, 40))
    put("swap", np.eye(P)[(np.arange(P) + 64) % P])
    p, q = np.arange(P)[:, None], np.arange(896)[None, :]
    put("mask", np.where(q <= p + 384, 0.0, NEG))
    r, m = np.arange(64)[:, None], np.arange(64)[None, :]
    put("same", (r // 8 == m // 8), 64)
    put("below", (r // 8 == m // 8) & (r < m), 64)
    put("newneg", np.where(r % 8 == 7, 0.0, NEG), 64)
    b8 = np.arange(8)[:, None]
    put("newrow", (m == 8 * b8 + 7), 8)
    put("newto", (r % 8 == 7) & (r // 8 == m // 8), 64)
    put("diag", (r // 8 == np.arange(8)[None, :]), 64)
    put("iota16", np.arange(16)[None, :])
    put("tok", np.arange(P)[:, None])
    put("row64", np.arange(P)[:, None] % 64)
    put("edge", np.array([[w / min(t + 1, w) for t in range(POOL_BUF)] for w in WINDOWS]).reshape(1, 60))
    ws = np.zeros((P, 4, 8))
    for b in range(NB):
        for g, w in enumerate(WINDOWS):
            ws[b * POOL_BUF + POOL_BUF - (w - 1):(b + 1) * POOL_BUF, g, b] = 1.0 / w
    put("wsel", ws.reshape(P, 32))
    lo, hi = CO["bits"]
    c.view(np.int32)[:, lo:hi] = 0
    for b in range(31):
        c.view(np.int32)[:, lo + b] = 1 << b
    return c


QI_T, XP_T, Q_T, PM_T, WO_T, GV_T = 0, 4, 8, 12, 16, 24
DN_T = GV_T + 2 * NF
TILES = DN_T + KD
EVAC_GATE = 24
EVAC_DN = EVAC_GATE + NF
EVACS = EVAC_DN + KD
C_WO, C_GV = 8, 12
C_DN = C_GV + NF
CHUNKS = C_DN + KD
CHUNK_DMAS = {0: 3, 1: 1, 2: 1, 3: 1, 4: 1, 5: 4, 6: 4, 7: 1, 8: 3, 9: 3, 10: 3, 11: 3}


def dmas_before(c):
    return sum(CHUNK_DMAS.get(i, 2 if i < C_DN else 1) for i in range(c % 2, c + 1, 2))


SLOT_DMAS = (dmas_before(CHUNKS - 2), dmas_before(CHUNKS - 1))
UNITS = NT * N_HEADS
BITS = 31


def build(nc, A, O, scratch):
    ctx = ExitStack()

    class Signal:

        def __init__(self, name, per):
            self.sem, self.per = ctx.enter_context(nc.semaphore(name)), per

        def __call__(self, rnd, n):
            return self.sem, rnd * self.per + n

    class Steps(Signal):

        def begin(self, rnd):
            self.rnd, self.n = rnd, 0

        def add(self, ins):
            ins.then_inc(self.sem, 1)
            self.n += 1

        def last(self):
            return self(self.rnd, self.n)

        def end(self):
            assert self.n == self.per, (self.sem, self.n)

    with ctx:
        def sb(name, shape, dt=F32):
            return ctx.enter_context(nc.sbuf_tensor(name, shape, dt))

        C = sb("C", [P, NCONST])

        def const(name, rows=P):
            lo, hi = CO[name]
            return C[0:rows, lo:hi]

        ident, ones = const("ident"), const("ones")
        xT = sb("xT", [P, KD, TOK])
        hT = sb("hT", [P, KD, TOK])
        moR = sb("moR", [P, KD * TOK])
        mo = moR[:, :].rearrange("p (k t) -> p k t", k=KD)
        yR = sb("yR", [P, NF * TOK])
        yT = yR[:, :].rearrange("p (k t) -> p k t", k=NF)
        W = sb("W", [P, 2, NF * P])
        vec_rows = sb("vec_rows", [P, P])
        V = sb("V", [P, P])
        state_rows = sb("state_rows", [P, 512])
        prevs = sb("prevs", [P, 32])
        conv_T = sb("conv_T", [P, NF, 16])
        NAT = sb("NAT", [P, 5, KVW])
        kid = sb("kid", [P, 5, 2, HD])
        kT = sb("kT", [P, TOK])
        kiT = sb("kiT", [P, TOK])
        WI = sb("WI", [P, 5, 8])
        QQ = sb("QQ", [P, 8 * TOK])
        qiT = QQ[:, 0:4 * TOK].rearrange("p (k t) -> p k t", k=4)
        qT = QQ[:, 4 * TOK:].rearrange("p (k t) -> p k t", k=4)
        conv_rows = QQ[0:16, 0:D_FF]
        QZ = sb("QZ", [P, 2, TOK])
        SQ = sb("SQ", [P, 4, TOK])
        RB = SQ[:, :, 0:SEQ]
        SQ0 = SQ[:, 0, :]
        ix = SQ0[0:16, 0:256].rearrange("p (w b i) -> p w b i", w=2, b=NB)
        ixf = SQ0[0:16, 256:384].rearrange("p (b i) -> p b i", b=NB)
        ixi = SQ0[0:16, 384:512].bitcast(I32).rearrange("p (b i) -> p b i", b=NB)
        sc2 = SQ[:, 1, 0:P]
        pT2 = SQ[:, 1, P:2 * P].rearrange("p (t c) -> p t c", t=2)
        QC = sb("QC", [P, 2, TOK])
        TS = sb("TS", [P, TOK])
        rstd = sb("rstd", [P, TOK])
        SEL = sb("SEL", [P, 3 * KEYS_ALL])
        SCT, WK, NOT = (SEL[:, i * KEYS_ALL:(i + 1) * KEYS_ALL] for i in range(3))
        M8 = sb("M8", [P, 8])
        XPb = sb("XPb", [P, 4, POOL_BUF + SEQ])
        XS = sb("XS", [P, 4, NB])
        G = SEL[:, 0:2 * 522].rearrange("p (a t) -> p a t", a=2)
        CV = SEL[:, 1044:1044 + 2 * TOK].rearrange("p (a t) -> p a t", a=2)
        GE = SEL[:, 2084:2084 + 2 * TOK].rearrange("p (a t) -> p a t", a=2)
        CVO = QQ[32:42, 0:D_FF]
        POUT, POUT2 = QZ[0:15, 0, 0:512], QZ[0:NB, 1, 0:512]
        S, S2, J, J2, SA, PA = (yR[0:64, 6144 + 257 * i:6401 + 257 * i] for i in range(6))
        posI = yR[:, 7686:8070].bitcast(I32).rearrange("p (a c) -> p a c", a=3)
        IK = yR[:, 0:64 * P].rearrange("p (j d) -> p j d", j=64)
        KG = yR[:, 0:16 * P].rearrange("p (j d) -> p j d", j=16)
        VG = yR[:, 2048:4096].rearrange("p (j d) -> p j d", j=16)
        KTS = yR[:, 4096:6144].rearrange("p (j d) -> p j d", j=16)
        DIFF = yR[:, 8192:8192 + 4 * TOK].rearrange("p (g t) -> p g t", g=4)
        OA = yR[:, 8192:9216].bitcast(BF16).rearrange("p (c i) -> p c i", i=16)
        OB = yR[:, 9216:11264].bitcast(BF16).rearrange("p (c w i) -> p c w i", w=2, i=16)
        LA = moR[:, 0:4 * 527].rearrange("p (g t) -> p g t", g=4)
        LB = moR[:, 2108:2108 + 3 * 527].rearrange("p (g t) -> p g t", g=3)
        KIS = moR[:, 0:1024].rearrange("p (a t) -> p a t", a=2)
        SW = moR[:, 1024:2048]
        ARS = moR[:, 0:1024].rearrange("p (a t) -> p a t", a=2)
        ARP = moR[:, 1024:3072].rearrange("p (a t) -> p a t", a=4)
        ART = moR[:, 3072:4096].rearrange("p (a t) -> p a t", a=2)
        att = sb("att", [P, 4, 4])
        PT = sb("PT", [P, NB, NPG], I32)
        idxI = sb("idxI", [P, NB, NPP], I32)
        phys = sb("phys", [P, 2, NB, NPP])
        base = sb("base", [P, 1])
        qib = sb("qib", [P, NB, 16])
        qb = sb("qb", [P, NB, 8])
        wdiag = sb("wdiag", [8, NB, 8])
        wbc = sb("wbc", [P, NB, 8])
        sdot = sb("sdot", [8, 64])
        snew = sb("snew", [8, 1])
        sTok = sb("sTok", [P, P])
        cols = sb("cols", [64, 16])
        sgn, kth, cntA, cntB, offs, need, snegc = (cols[:, i:i + 1] for i in range(7))
        candI = sb("candI", [64, 2], I32)
        IDX = sb("IDX", [P, NB, 2], I32)
        sm = sb("sm", [64, 8])
        pnd = sb("pnd", [64, 8])
        tmp8 = sb("tmp8", [64, 8])
        pn = sb("pn", [8, 64])

        ps = ctx.enter_context(nc.psum_tensor("ps", [P, 8, 512], F32))

        def main(g):
            return ps[:, 2 * (g % 2):2 * (g % 2) + 2, 0:HT]

        def halves(ap):
            return ap.rearrange("p (f t) -> p f t", f=2)

        const_in = Signal("const_in", 0)
        x_in = Signal("x_in", 0)
        x_turned = Signal("x_turned", 0)
        w_in_slot = [Signal("w_in_slot0", 16 * SLOT_DMAS[0]), Signal("w_in_slot1", 16 * SLOT_DMAS[1])]
        vec_in = Signal("vec_in", 16 * 9)
        pages_in = Signal("pages_in", 16 * 64)
        prep_mm = Signal("prep_mm", 1)
        prep_ev = Signal("prep_ev", 3)
        x_ready = Signal("x_ready", 16)
        sq_ready = Signal("sq_ready", 16)
        sq_used = Signal("sq_used", 32)
        var_ready = Signal("var_ready", 8)
        root_ready = Signal("root_ready", 8)
        rstd_ready = Signal("rstd_ready", 8)
        h_ready = Signal("h_ready", 16)
        kv_mm = Signal("kv_mm", 5)
        kv_ev = Signal("kv_ev", 5)
        nat_ready = Signal("nat_ready", 2)
        kid_ready = Signal("kid_ready", 1)
        kt_mm = Signal("kt_mm", 3)
        kt_ev = Signal("kt_ev", 4)
        tile_done = Signal("tile_done", TILES)
        evac = Signal("evac", EVACS)
        val_used = Signal("val_used", NF)
        rot_mm = Signal("rot_mm", 8)
        qc_ready = Signal("qc_ready", 8)
        rot_used = Signal("rot_used", 8)
        rope_done = Signal("rope_done", 8)
        dot_mm = Signal("dot_mm", 24)
        dot_relu = Signal("dot_relu", 24)
        dot_acc = Signal("dot_acc", 24)
        sel_ready = Signal("sel_ready", 3)
        qib_mm = Signal("qib_mm", 2)
        qib_ev = Signal("qib_ev", 7)
        wd_ready = Signal("wd_ready", 1)
        pg_mm = Signal("pg_mm", 16)
        pg_ev = Signal("pg_ev", 16)
        sdot_mm = Signal("sdot_mm", 17)
        sw_used = Signal("sw_used", 9)
        stok_ready = Signal("stok_ready", 2)
        sT_mm = Signal("sT_mm", 2)
        sT_ev = Signal("sT_ev", 1)
        cnt_ready = Signal("cnt_ready", 1 + BITS)
        cnt_mm = Signal("cnt_mm", 1 + BITS)
        pick_ready = Signal("pick_ready", 4)
        pick_mm = Signal("pick_mm", 4)
        pos_mm = Signal("pos_mm", 1)
        hot_ready = Signal("hot_ready", 1)
        list_mm = Signal("list_mm", 1)
        list_ev = Signal("list_ev", 1)
        list_ready = Signal("list_ready", 1)
        list_out = Signal("list_out", 16)
        list_in = Signal("list_in", 16)
        kg_in = Signal("kg_in", 16 * 16)
        vg_in = Signal("vg_in", 16 * 16)
        tables = Signal("tables", 0)
        sums_ready = Signal("sums_ready", 4)
        diff_ready = Signal("diff_ready", 8)
        pout_mm = Signal("pout_mm", 1)
        pout_ev = Signal("pout_ev", 1)
        qk_mm = Signal("qk_mm", UNITS)
        qk_used = Signal("qk_used", UNITS)
        neg_max = Signal("neg_max", UNITS)
        exp_done = Signal("exp_done", UNITS)
        prob_ready = Signal("prob_ready", UNITS)
        pt_mm = Signal("pt_mm", UNITS)
        pt_ev = Signal("pt_ev", UNITS)
        pv_mm = Signal("pv_mm", UNITS)
        o_ev = Signal("o_ev", NT)
        ks_mm = Signal("ks_mm", 4)
        ks_ev = Signal("ks_ev", 4)
        qs_mm = Signal("qs_mm", 3)
        qs_ev = Signal("qs_ev", 2)
        ss_ready = Signal("ss_ready", 1)
        se_ready = Signal("se_ready", 1)
        sp_ready = Signal("sp_ready", 2)
        sp_mm = Signal("sp_mm", 1)
        sp_ev = Signal("sp_ev", 2)
        so_mm = Signal("so_mm", 1)
        so_ev = Signal("so_ev", 2)
        upd = Signal("upd", 16)
        conv_done = Signal("conv_done", NF)
        gelu_done = Signal("gelu_done", NF)
        y_ready = val_used
        co_mm = Signal("co_mm", NF)
        co_ev = Signal("co_ev", NF)
        out_sync = Signal("out_sync", 16 * 12)
        y_mm = Signal("y_mm", 0)
        y_ev = Signal("y_ev", 0)
        y_out = Signal("y_out", 0)
        dve_step = Steps("dve_step", 229)
        passed = {e.engine: Signal(f"passed{i}", 0) for i, e in
                  enumerate((nc.sync, nc.gpsimd, nc.tensor, nc.scalar, nc.vector))}
        ffn_step = Steps("ffn_step", 4)
        pool_step = Signal("pool_step", 1)

        def gain(a, k):
            return V[:, 8 * a + k:8 * a + k + 1]
        G_PRE_MIX, G_POST_MIX, G_PRE_FFN, G_POST_FFN = range(4)

        def wslot(c):
            return W[:, c % 2, :]

        def pair_w(c):
            return wslot(c)[:, 0:2048].rearrange("p (k n) -> p k n", k=KD)

        x_rows = yR[:, 0:NT * D_MODEL].rearrange("p (t d) -> p t d", t=NT)
        xs_rows = yR[0:NB, 4096:4096 + D_MODEL]

        def wait_alone(eng, sem, value):
            eng.wait_ge(sem, value)
            eng.sem_inc(passed[eng.engine].sem, 1)

        block = ctx.enter_context(nc.Block())

        @block.sync
        def _(sp):
            sp.dma_start(C[:, :], A["consts"]).then_inc(const_in.sem, 16)
            sp.dma_start(PT[:, :, :].rearrange("p b j -> p (b j)"),
                         A["page_table"].rearrange("b j -> (b j)").partition_broadcast(P)).then_inc(const_in.sem, 16)
            sp.dma_start(x_rows, A["x_prompt"][0].rearrange("(t p) d -> p t d", p=P)).then_inc(x_in.sem, 16)
            sp.dma_start(xs_rows, A["x_sample"][:, 0, :]).then_inc(x_in.sem, 16)

            def layer(l):
                w_in = A["w_in"][l].rearrange("(k p) n -> p k n", p=P)

                def load(c):
                    s = w_in_slot[c % 2].sem
                    if c == 0:
                        d = wslot(0)[:, 0:KD * KVW].rearrange("p (k n) -> p k n", k=KD)
                        sp.dma_start(d[:, :, 0:128], w_in[:, :, K0:K0 + 128]).then_inc(s, 16)
                        sp.dma_start(d[:, :, 128:200], w_in[:, :, KI0:KI0 + 72]).then_inc(s, 16)
                        sp.dma_start(d[:, :, 200:328], w_in[:, :, V0:V0 + 128]).then_inc(s, 16)
                    elif c < 5:
                        c0 = (QI0 if c < 3 else XP0) + 256 * ((c - 1) % 2)
                        sp.dma_start(pair_w(c), w_in[:, :, c0:c0 + 256]).then_inc(s, 16)
                    elif c < 7:
                        for u in range(2):
                            for n in range(2):
                                c0 = Q0 + 256 * n + HD * (2 * (c - 5) + u)
                                d = P * u + HD * n
                                sp.dma_start(pair_w(c)[:, :, d:d + HD], w_in[:, :, c0:c0 + HD]).then_inc(s, 16)
                    elif c == 7:
                        sp.dma_start(wslot(7)[:, 0:512].rearrange("p (g d) -> p g d", g=4),
                                     A["w_pool"][l].rearrange("g c d -> c g d")).then_inc(s, 16)
                    else:
                        c0 = 256 * (c - C_WO)
                        w = A["w_out"][l][:, c0:c0 + 256]
                        d = pair_w(c)
                        for n in range(2):
                            sp.dma_start(d[64 * n:64 * n + 64, 0:4, :],
                                         w[256 * n:256 * n + 256, :].rearrange("(j d) n -> d j n", j=4)
                                         ).then_inc(s, 16)
                        sp.dma_start(d[:, 4:8, :], w[512:1024, :].rearrange("(k p) n -> p k n", p=P)
                                     ).then_inc(s, 16)

                wait_alone(sp, *so_ev(l, 0))
                v = vec_rows
                for a, name in enumerate(("g_pre_mix", "g_post_mix", "g_pre_ffn", "g_post_ffn")):
                    sp.dma_start(v[8 * a:8 * a + 8, :], A[name][l].rearrange("(k p) -> k p", p=P)
                                 ).then_inc(vec_in.sem, 16)
                sp.dma_start(v[32:36, :], A["pool_scale"][l].rearrange("(k p) -> k p", p=P)
                             ).then_inc(vec_in.sem, 16)
                sp.dma_start(v[36:102, :], A["conv_w"][l].rearrange("j (k p) -> (j k) p", p=P)
                             ).then_inc(vec_in.sem, 16)
                sp.dma_start(v[102:124, :], A["conv_b"][l].rearrange("(k p) -> k p", p=P)).then_inc(vec_in.sem, 16)
                sp.dma_start(state_rows[0:NB * POOL_BUF, :], A["state_pool"][l].rearrange("b r c -> (b r) c")
                             ).then_inc(vec_in.sem, 16)
                sp.dma_start(conv_rows, A["state_conv"][l].rearrange("b j f -> (b j) f")).then_inc(vec_in.sem, 16)
                wait_alone(sp, *tile_done(l, 0))
                load(0)
                load(1)
                wait_alone(sp, *kv_mm(l, 5))
                load(2)
                for c in (3, 4):
                    wait_alone(sp, *tile_done(l, 2 * (c - 2)))
                    load(c)
                wait_alone(sp, *nat_ready(l, 1))
                for t, name in ((0, "prompt"), (4, "sample")):
                    if t == 0:
                        kvd = [O[f"new_{x}_prompt"][l, 0].rearrange("(t p) n d -> p t (n d)", p=P) for x in "kv"]
                        kid_d = O["new_ik_prompt"][l, 0].rearrange("(t p) d -> p t d", p=P)
                        src = NAT[:, 0:4, :]
                    else:
                        kvd = [O[f"new_{x}_sample"][l, :, 0].rearrange("b n d -> b (n d)") for x in "kv"]
                        kid_d = O["new_ik_sample"][l, :, 0]
                        src = NAT[0:NB, 4, :]
                    at = (lambda a, b: src[:, :, a:b]) if t == 0 else (lambda a, b: src[:, a:b])
                    sp.dma_start(kvd[0], at(0, 128)).then_inc(out_sync.sem, 16)
                    sp.dma_start(kvd[1], at(200, 328)).then_inc(out_sync.sem, 16)
                    sp.dma_start(kid_d, at(128, 192)).then_inc(out_sync.sem, 16)
                for c in (5, 6, 7):
                    wait_alone(sp, *tile_done(l, 2 * (c - 2)))
                    load(c)
                wait_alone(sp, *tile_done(l, PM_T))
                load(8)
                sp.dma_start(O["new_pool_sample"][l, :, 0:14, :], A["state_pool"][l, :, 1:15, :]
                             ).then_inc(out_sync.sem, 16)
                sp.dma_start(O["new_conv_sample"][l, :, 0, :], A["state_conv"][l, :, 1, :]
                             ).then_inc(out_sync.sem, 16)
                wait_alone(sp, *pout_ev(l, 1))
                sp.dma_start(O["new_pool_prompt"][l, 0], POUT[0:15, :]).then_inc(out_sync.sem, 16)
                sp.dma_start(O["new_pool_sample"][l, :, 14, :], POUT2[:, :]).then_inc(out_sync.sem, 16)
                wait_alone(sp, *tile_done(l, WO_T))
                load(9)
                for c in (10, 11):
                    wait_alone(sp, *tile_done(l, WO_T + 2 * (c - 9)))
                    load(c)

                def gate_value(i, slot):
                    d = W[:, slot, 0:2048].rearrange("p (a k n) -> p a k n", a=2, k=KD)
                    for a, name in enumerate(("w_gate", "w_val")):
                        sp.dma_start(d[:, a], A[name][l].rearrange("(k p) (i n) -> p k i n", p=P, n=P)[:, :, i, :]
                                     ).then_inc(w_in_slot[slot].sem, 16)
                wait_alone(sp, *tile_done(l, WO_T + 6))
                gate_value(0, 0)
                wait_alone(sp, *tile_done(l, WO_T + 8))
                gate_value(1, 1)
                with sp.Fori(1, NF // 2) as i:
                    for u in range(2):
                        wait_alone(sp, tile_done.sem, l * TILES + i * 4 + (GV_T - 4 + 2 * u + 2))
                        gate_value(i * 2 + u, u)
                with sp.Fori(0, KD // 2) as m:
                    for u in range(2):
                        wait_alone(sp, tile_done.sem, l * TILES + m * 2 + (DN_T - 1 + u))
                        sp.dma_start(wslot(u)[:, :].rearrange("p (k n) -> p k n", k=NF),
                                     A["w_down"][l].rearrange("(k p) (m n) -> p k m n", p=P, n=P)[:, :, m * 2 + u, :]
                                     ).then_inc(w_in_slot[u].sem, 16)
                wait_alone(sp, *co_ev(l, NF))
                sp.dma_start(O["new_conv_prompt"][l, 0], CVO[0:2, :]).then_inc(out_sync.sem, 16)
                sp.dma_start(O["new_conv_sample"][l, :, 1, :], CVO[2:10, :]).then_inc(out_sync.sem, 16)

            with sp.Fori(0, DEPTH) as l:
                layer(l)
            for t in range(NT):
                wait_alone(sp, *y_ev(0, 2 * t + 2))
                sp.dma_start(O["y_prompt"][0, t * P:(t + 1) * P, :], x_rows[:, t, :]).then_inc(y_out.sem, 16)
            wait_alone(sp, *y_ev(0, 10))
            sp.dma_start(O["y_sample"][:, 0, :], xs_rows).then_inc(y_out.sem, 16)
            sp.wait_ge(y_out.sem, 16 * 5)
            sp.wait_ge(out_sync.sem, 16 * 12 * DEPTH)

        @block.gpsimd
        def _(gp):
            page_pairs = A["cache_idx_k"].rearrange("l n (r e) d -> (l n r) (e d)", e=2)
            k_rows = A["cache_k"].rearrange("l n r h d -> (l n r) (h d)")
            v_rows = A["cache_v"].rearrange("l n r h d -> (l n r) (h d)")
            gp.wait_ge(tables.sem, 3)
            gp.wait_ge(x_turned.sem, KD)

            def cos_part(l, j):
                wait_alone(gp, *evac(l, (QI_T if j < 4 else Q_T - 4) + j + 1))
                if j >= 2:
                    wait_alone(gp, *rope_done(l, j - 1))
                nc.gpsimd.tensor_tensor(QC[:, j % 2, :], QZ[:, j % 2, :], const("cosT"), ALU.mult
                                        ).then_inc(qc_ready.sem, 1)

            def add_updates(l, at):
                for k in range(KD):
                    wait_alone(gp, *upd(l, at + k + 1))
                    nc.gpsimd.tensor_tensor(xT[:, k, :], xT[:, k, :], mo[:, k, :], ALU.add
                                            ).then_inc(x_ready.sem, 1)

            def layer(l):
                wait_alone(gp, *tile_done(l, 0))
                if DEPTH > 1:
                    wait_alone(gp, *pages_in(l, 0))
                for j in range(64):
                    nc.gpsimd.indirect_dma_start(
                        IK[:, j, :], None, page_pairs,
                        bass.IndirectOffsetOnAxis(ap=idxI[:, j // NPP, j % NPP:j % NPP + 1], axis=0)
                    ).then_inc(pages_in.sem, 16)
                for j in range(4):
                    cos_part(l, j)
                wait_alone(gp, *evac(l, Q_T))
                wait_alone(gp, *stok_ready(l, 2))
                wait_alone(gp, *sdot_mm(l, 17))
                nc.gpsimd.tensor_tensor(LA[:, :, 1:527], XPb[:, :, 1:527], XPb[:, :, 0:526], ALU.add
                                        ).then_inc(sums_ready.sem, 1)
                wait_alone(gp, *sums_ready(l, 1))
                nc.gpsimd.tensor_tensor(LB[:, :, 3:527], LA[:, 1:4, 3:527], LA[:, 1:4, 1:525], ALU.add
                                        ).then_inc(sums_ready.sem, 1)
                wait_alone(gp, *sums_ready(l, 2))
                nc.gpsimd.tensor_tensor(LA[:, 2:4, 7:527], LB[:, 1:3, 7:527], LB[:, 1:3, 3:523], ALU.add
                                        ).then_inc(sums_ready.sem, 1)
                wait_alone(gp, *sums_ready(l, 3))
                nc.gpsimd.tensor_tensor(LB[:, 2, 15:527], LA[:, 3, 15:527], LA[:, 3, 7:519], ALU.add
                                        ).then_inc(sums_ready.sem, 1)
                for j in range(4, 8):
                    cos_part(l, j)
                wait_alone(gp, *pages_in(l, 16 * 64))
                nc.gpsimd.tensor_scalar(idxI[:, :, :], idxI[:, :, :], float(N_PHYS * 64), None, ALU.add
                                        ).then_inc(pool_step.sem, 1)
                wait_alone(gp, *list_ready(l, 1))
                gp.dma_start(scratch.rearrange("b (h i) -> h b i", h=16), ixi[:, :, :]).then_inc(list_out.sem, 16)
                wait_alone(gp, *list_out(l, 16))
                gp.dma_start(IDX[:, :, :], scratch.rearrange("b (p t) -> p b t", t=2)).then_inc(list_in.sem, 16)
                wait_alone(gp, *list_in(l, 16))
                for dst, rows, s in ((KG, k_rows, kg_in), (VG, v_rows, vg_in)):
                    for b in range(NB):
                        for t in range(2):
                            nc.gpsimd.indirect_dma_start(
                                dst[:, 2 * b + t, :], None, rows,
                                bass.IndirectOffsetOnAxis(ap=IDX[:, b, t:t + 1], axis=0)).then_inc(s.sem, 16)
                add_updates(l, 0)
                wait_alone(gp, *pool_step(l, 1))
                add_updates(l, KD)

            with gp.Fori(0, DEPTH) as l:
                layer(l)

        @block.tensor
        def _(pe):
            mm, turn = nc.tensor.matmul, nc.tensor.transpose

            pe.wait_ge(const_in.sem, 32)
            pe.wait_ge(x_in.sem, 32)
            for k in range(KD):
                if k >= 2:
                    pe.wait_ge(x_ready.sem, k - 1)
                b = 2 * (k % 2)
                for t in range(NT):
                    turn(ps[:, b, t * P:(t + 1) * P], x_rows[:, t, k * P:(k + 1) * P], ident)
                turn(ps[:, b + 1, 0:NB], xs_rows[:, k * P:(k + 1) * P], ident[0:NB, 0:NB]
                     ).then_inc(x_turned.sem, 1)

            def squares(l, n, k):
                for f in range(2):
                    last = mm(ps[:, 4 + f, 0:HT], ones, SQ[:, k % 4, f * HT:(f + 1) * HT],
                              start=(k == 0), stop=(k == KD - 1))
                last.then_inc(sq_used.sem, 1)

            def arrived(l, c):
                pe.wait_ge(*w_in_slot[c % 2](l, 16 * dmas_before(c)))

            def product(g, lhsT, rhs, nk, extras=None, before=None):
                for k in range(nk):
                    if before:
                        before(k)
                    for f in range(2):
                        last = mm(ps[:, 2 * (g % 2) + f, 0:HT], lhsT(k), rhs[:, k, f * HT:(f + 1) * HT],
                                  start=(k == 0), stop=(k == nk - 1))
                    if extras and k % 2 == 1 and k < nk - 1:
                        extras.pop(0)()
                last.then_inc(tile_done.sem, 1)
                if extras:
                    extras.pop(0)()

            def layer(l):
                pe.wait_ge(*vec_in(l, 16 * 9))
                pe.wait_ge(*co_ev(l, 0))
                turn(ps[:, 7, 0:124], vec_rows[0:124, :], ident[0:124, 0:124])
                rows = NB * POOL_BUF
                for g in range(4):
                    mm(ps[:, 7, P + 8 * g:P + 8 * g + 8], state_rows[0:rows, g * P:(g + 1) * P],
                       const("wsel", rows)[:, 8 * g:8 * g + 8], start=True, stop=True)
                for i in range(NF):
                    last = turn(ps[:, 6, 16 * i:16 * i + 16], conv_rows[:, i * P:(i + 1) * P], ident[0:16, 0:16])
                last.then_inc(prep_mm.sem, 1)
                for k in range(KD):
                    pe.wait_ge(*sq_ready(l, k + 1))
                    squares(l, 0, k)
                arrived(l, 0)
                wkv = wslot(0)[:, 0:KD * KVW].rearrange("p (k n) -> p k n", k=KD)
                for t in range(5):
                    m, bank = (P, t) if t < NT else (NB, 6)
                    pe.wait_ge(*(evac(l, 0) if t < NT else prep_ev(l, 3)))
                    for k in range(KD):
                        if t == 0:
                            pe.wait_ge(*h_ready(l, k + 1))
                        last = mm(ps[0:m, bank, 0:KVW], hT[:, k, t * P:t * P + m], wkv[:, k, :],
                                  start=(k == 0), stop=(k == KD - 1))
                    last.then_inc(kv_mm.sem, 1)

                def tile8(g, c, u, rhs=hT, **kw):
                    product(g, lambda k: pair_w(c)[:, k, u * P:(u + 1) * P], rhs, KD, **kw)

                def partner(j):
                    pe.wait_ge(*evac(l, (QI_T if j < 4 else Q_T - 4) + j + 1))
                    if j == 0:
                        pe.wait_ge(*kv_ev(l, 5))
                        pe.wait_ge(*kt_ev(l, 4))
                    elif j == 4:
                        pe.wait_ge(*sw_used(l, 8))
                    else:
                        pe.wait_ge(*rot_used(l, j))
                    for f in range(2):
                        last = mm(ps[:, 6 + f, 0:HT], const("rot"), QZ[:, j % 2, f * HT:(f + 1) * HT],
                                  start=True, stop=True)
                    last.then_inc(rot_mm.sem, 1)

                for j in range(4):
                    if j % 2 == 0:
                        arrived(l, 1 + j // 2)
                    pe.wait_ge(*(kv_ev(l, 2 + 2 * j) if j < 2 else evac(l, j - 1)))
                    tile8(QI_T + j, 1 + j // 2, j % 2)
                    if j == 1:
                        pe.wait_ge(*kid_ready(l, 1))
                        pe.wait_ge(*prep_ev(l, 3))
                        for t in range(NT):
                            last = turn(ps[:, 4, t * P:(t + 1) * P],
                                        kid[:, t, :, :].rearrange("p a d -> p (a d)"), ident)
                        last.then_inc(kt_mm.sem, 1)
                        for t in range(NT):
                            last = turn(ps[:, 5, t * P:(t + 1) * P], NAT[:, t, 0:P], ident)
                        last.then_inc(kt_mm.sem, 1)
                        turn(ps[:, 7, 0:NB], kid[0:NB, 4, :, :].rearrange("p a d -> p (a d)"), ident[0:NB, 0:NB])
                        turn(ps[:, 7, 8:8 + NB], NAT[0:NB, 4, 0:P], ident[0:NB, 0:NB]).then_inc(kt_mm.sem, 1)
                        partner(0)
                    elif j >= 2:
                        partner(j - 1)
                partner(3)

                for d in range(24):
                    t, h = 1 + d // 8, d % 8
                    if d == 0:
                        pe.wait_ge(*rope_done(l, 4))
                        pe.wait_ge(*kt_ev(l, 4))
                    if d >= 2:
                        pe.wait_ge(*dot_relu(l, d - 1))
                    rows = slice(64 * (h % 2), 64 * (h % 2) + 64)
                    mm(ps[:, 4 + d % 2, 0:P * (t + 1)], qiT[rows, h // 2, t * P:(t + 1) * P],
                       kiT[rows, 0:P * (t + 1)], start=True, stop=True).then_inc(dot_mm.sem, 1)

                pe.wait_ge(*rot_used(l, 4))
                mm(ps[:, 6, 0:32], const("swap"), qiT[:, 0:4, SEQ:TOK], start=True, stop=True
                   ).then_inc(qib_mm.sem, 1)
                pe.wait_ge(*wd_ready(l, 1))
                mm(ps[:, 7, 0:64], ones[0:8, :], wdiag[:, :, :].rearrange("p b h -> p (b h)"),
                   start=True, stop=True).then_inc(qib_mm.sem, 1)

                def page_products(g):
                    pe.wait_ge(*pg_ev(l, g + 1))
                    for i in range(4):
                        q = 4 * g + i
                        last = mm(ps[:, 6 + q // 32, 16 * (q % 32):16 * (q % 32) + 16],
                                  KIS[:, g % 2, i * P:(i + 1) * P], qib[:, q // NPP, :], start=True, stop=True)
                    last.then_inc(sdot_mm.sem, 1)

                pe.wait_ge(*pages_in(l, 16 * 64))
                for g in range(16):
                    pe.wait_ge(*(dot_relu(l, 23 + g) if g < 2 else pg_ev(l, g - 1)))
                    for i in range(4):
                        last = turn(ps[:, 4 + g % 2, i * P:(i + 1) * P], IK[:, 4 * g + i, :], ident)
                    last.then_inc(pg_mm.sem, 1)
                    if g == 1:
                        pe.wait_ge(*qib_ev(l, 5))
                    if g >= 1:
                        page_products(g - 1)
                page_products(15)
                mm(ps[0:NB, 4, 0:64], kiT[0:64, SEQ:TOK], qib[0:64, :, 0:8], start=True, stop=True
                   ).then_inc(sdot_mm.sem, 1)

                for j in range(4):
                    if j % 2 == 0:
                        arrived(l, 3 + j // 2)
                    pe.wait_ge(*evac(l, XP_T + j - 1))
                    tile8(XP_T + j, 3 + j // 2, j % 2)

                def scores_turned():
                    wait_alone(pe, *stok_ready(l, 2))
                    for e in range(2):
                        last = turn(ps[0:64, 4, e * P:(e + 1) * P], sTok[:, e:P:2], ident)
                    last.then_inc(sT_mm.sem, 1)
                    mm(ps[0:64, 5, 0:1], const("newrow", 8), snew[:, :], start=True, stop=True
                       ).then_inc(sT_mm.sem, 1)

                def count(s):
                    def go():
                        wait_alone(pe, *cnt_ready(l, s + 1))
                        mm(ps[0:64, 4 + s % 2, 300:301], const("same", 64), (cntB if s % 2 else cntA),
                           start=True, stop=True).then_inc(cnt_mm.sem, 1)
                    return go

                extras = [scores_turned] + [count(s) for s in range(1 + BITS)]
                for j in range(4):
                    if j % 2 == 0:
                        arrived(l, 5 + j // 2)
                    pe.wait_ge(*evac(l, Q_T + j - 1))
                    tile8(Q_T + j, 5 + j // 2, j % 2, extras=extras)
                    if j >= 1:
                        partner(3 + j)
                partner(7)
                pe.wait_ge(*rot_used(l, 8))
                for g in range(4):
                    turn(ps[0:15, 6, g * P:(g + 1) * P], XPb[:, g, 512:527], ident)
                for g in range(4):
                    last = turn(ps[0:NB, 7, g * P:(g + 1) * P], XS[:, g, :], ident)
                last.then_inc(pout_mm.sem, 1)
                arrived(l, 7)
                wp = wslot(7)[:, 0:512].rearrange("p (g d) -> p g d", g=4)
                for g in range(4):
                    pe.wait_ge(*evac(l, PM_T + g - 1))
                    pe.wait_ge(*diff_ready(l, 2 * g + 2))
                    for f in range(2):
                        last = mm(ps[:, 2 * (g % 2) + f, 0:HT], wp[:, g, :], DIFF[:, g, f * HT:(f + 1) * HT],
                                  start=True, stop=True)
                    last.then_inc(tile_done.sem, 1)
                    for _ in range(3):
                        if extras:
                            extras.pop(0)()
                while extras:
                    extras.pop(0)()

                def pick_a():
                    wait_alone(pe, *pick_ready(l, 2))
                    wait_alone(pe, *evac(l, WO_T))
                    mm(ps[0:64, 3, 0:1], const("same", 64), cntA, start=True, stop=True).then_inc(pick_mm.sem, 1)
                    mm(ps[0:64, 3, 1:2], const("below", 64), cntB, start=True, stop=True).then_inc(pick_mm.sem, 1)

                def pick_b():
                    wait_alone(pe, *pick_ready(l, 3))
                    mm(ps[0:64, 3, 2:3], const("below", 64), cntA, start=True, stop=True).then_inc(pick_mm.sem, 1)
                    mm(ps[0:64, 3, 3:4], const("newto", 64), J[:, 256:257], start=True, stop=True
                       ).then_inc(pick_mm.sem, 1)

                def pick_c():
                    wait_alone(pe, *pick_ready(l, 4))
                    for g in range(2):
                        last = turn(ps[:, 3, P + 64 * g:P + 64 * g + 64], S2[:, g * P:(g + 1) * P],
                                    ident[0:64, 0:64])
                    last.then_inc(pos_mm.sem, 1)

                def pick_d():
                    wait_alone(pe, *hot_ready(l, 1))
                    for b in range(NB):
                        for g in range(2):
                            for pp in range(NPP):
                                c = 64 * g + NPP * b + pp
                                last = mm(ps[0:16, 3, 256 + 32 * b:288 + 32 * b], OA[:, c, :],
                                          OB[:, c, :, :].rearrange("p w i -> p (w i)"),
                                          start=(g == 0 and pp == 0), stop=(g == 1 and pp == NPP - 1))
                    last.then_inc(list_mm.sem, 1)

                picks = {1: pick_a, 3: pick_b, 5: pick_c, 9: pick_d}

                def scores(i):
                    t, h = divmod(i, N_HEADS)
                    rows = slice(64 * (h // 4), 64 * (h // 4) + 64)
                    if i == 0:
                        pe.wait_ge(*rope_done(l, 8))
                        pe.wait_ge(*evac(l, WO_T))
                    if i >= 3:
                        pe.wait_ge(*qk_used(l, i - 2))
                    mm(ps[:, i % 3, 0:P * (t + 1)], qT[rows, h % 4, t * P:(t + 1) * P],
                       kT[rows, 0:P * (t + 1)], start=True, stop=True).then_inc(qk_mm.sem, 1)

                def turn_probs(i):
                    t = i // N_HEADS
                    pe.wait_ge(*prob_ready(l, i + 1))
                    if i >= 2:
                        pe.wait_ge(*pt_ev(l, i - 1))
                    for kt in range(t + 1):
                        last = turn(ps[:, 4 + i % 2, kt * P:(kt + 1) * P], ARP[:, i % 4, kt * P:(kt + 1) * P], ident)
                    last.then_inc(pt_mm.sem, 1)

                def values(i):
                    t, h = divmod(i, N_HEADS)
                    n, j = divmod(h, 4)
                    pe.wait_ge(*pt_ev(l, i + 1))
                    if i == 0:
                        pe.wait_ge(*pout_ev(l, 1))
                    if h == 0 and t >= 2:
                        pe.wait_ge(*o_ev(l, t - 1))
                    for kt in range(t + 1):
                        last = mm(ps[64 * n:64 * n + 64, 6 + t % 2, j * P:(j + 1) * P],
                                  NAT[:, kt, 200 + 64 * n:264 + 64 * n], ART[:, i % 2, kt * P:(kt + 1) * P],
                                  start=(kt == 0), stop=(kt == t))
                    last.then_inc(pv_mm.sem, 1)

                for i in range(UNITS + 3):
                    if i < UNITS:
                        scores(i)
                    if i in picks:
                        picks[i]()
                    if 2 <= i < UNITS + 2:
                        turn_probs(i - 2)
                    if i >= 3:
                        values(i - 3)

                wait_alone(pe, *kg_in(l, 16 * 16))
                for q in range(4):
                    wait_alone(pe, *(list_ev(l, 1) if q == 0 else ks_ev(l, q)))
                    for i in range(4):
                        last = turn(ps[:, 3, i * P:(i + 1) * P], KG[:, 4 * q + i, :], ident)
                    last.then_inc(ks_mm.sem, 1)
                wait_alone(pe, *ks_ev(l, 4))
                wait_alone(pe, *qib_ev(l, 7))
                for b in range(NB):
                    for t in range(2):
                        last = mm(ps[:, 3, 64 * t + 8 * b:64 * t + 8 * b + 8], KTS[:, 2 * b + t, :], qb[:, b, :],
                                  start=True, stop=True)
                last.then_inc(qs_mm.sem, 1)
                wait_alone(pe, *qs_ev(l, 1))
                for t in range(2):
                    last = turn(ps[0:64, 3, P * (t + 1):P * (t + 2)], sc2[:, 64 * t:64 * t + 64], ident)
                last.then_inc(qs_mm.sem, 1)
                mm(ps[0:64, 3, 400:408], qb[:, :, :].rearrange("p b h -> p (b h)"), kT[:, SEQ:TOK],
                   start=True, stop=True).then_inc(qs_mm.sem, 1)
                wait_alone(pe, *sp_ready(l, 2))
                for t in range(2):
                    turn(ps[:, 3, 64 * t:64 * t + 64], PA[:, P * t:P * (t + 1)], ident[0:64, 0:64])
                turn(ps[0:8, 3, P:P + 64], pnd[:, :], ident[0:64, 0:64]).then_inc(sp_mm.sem, 1)
                wait_alone(pe, *sp_ev(l, 2))
                wait_alone(pe, *vg_in(l, 16 * 16))
                mm(ps[:, 3, 256:320], NAT[0:NB, 4, 200:328], pn[:, :], start=True, stop=False,
                   skip_group_check=True)
                for b in range(NB):
                    for t in range(2):
                        last = mm(ps[:, 3, 256 + 8 * b:264 + 8 * b], VG[:, 2 * b + t, :],
                                  pT2[:, t, 8 * b:8 * b + 8], start=False,
                                  stop=(b == NB - 1 and t == 1), skip_group_check=True)
                last.then_inc(so_mm.sem, 1)

                pe.wait_ge(*o_ev(l, NT))
                pe.wait_ge(*so_ev(l, 2))
                pe.wait_ge(*qk_used(l, UNITS))
                for m in range(KD):
                    if m % 2 == 0:
                        arrived(l, C_WO + m // 2)
                    if m >= 2:
                        pe.wait_ge(*evac(l, WO_T + m - 1))
                        squares(l, 1, m - 2)
                    tile8(WO_T + m, C_WO + m // 2, m % 2)
                for k in (6, 7):
                    pe.wait_ge(*evac(l, WO_T + k + 1))
                    squares(l, 1, k)
                for k in range(KD):
                    pe.wait_ge(*sq_ready(l, KD + k + 1))
                    squares(l, 2, k)

                def gate_value(i, r, u, first):
                    slot = w_in_slot[u]
                    pe.wait_ge(slot.sem, l * slot.per + r * 32 + 16 * (dmas_before(C_GV - 2 + u) + 2))
                    w = W[:, u, 0:2048].rearrange("p (a k n) -> p a k n", a=2, k=KD)

                    def h_there(k):
                        pe.wait_ge(*h_ready(l, KD + k + 1))
                    pe.wait_ge(*evac(l, i + EVAC_GATE))
                    product(0, lambda k: w[:, 0, k, :], hT, KD, before=h_there if first and u == 0 else None)
                    if first and u == 0:
                        pe.wait_ge(*evac(l, GV_T))
                    else:
                        pe.wait_ge(*val_used(l, i))
                    product(1, lambda k: w[:, 1, k, :], hT, KD)
                    pe.wait_ge(*evac(l, i + EVAC_GATE + 1))
                    if not first:
                        pe.wait_ge(*co_ev(l, i - 1))
                    turn(ps[0:10, 6 + u, 0:P], G[:, u, 512:522], ident).then_inc(co_mm.sem, 1)

                for u in range(2):
                    gate_value(u, 0, u, True)
                with pe.Fori(1, NF // 2) as r:
                    for u in range(2):
                        gate_value(r * 2 + u, r, u, False)

                for m in range(KD):
                    arrived(l, C_DN + m)
                    if m < 2:
                        pe.wait_ge(*val_used(l, NF))
                        pe.wait_ge(*evac(l, EVAC_DN))
                    else:
                        pe.wait_ge(*evac(l, EVAC_DN + m - 1))
                        squares(l, 3, m - 2)
                    c = C_DN + m
                    product(DN_T + m, lambda k: wslot(c)[:, k * P:(k + 1) * P], yT, NF)
                for k in (6, 7):
                    pe.wait_ge(*evac(l, EVAC_DN + k + 1))
                    squares(l, 3, k)

            with pe.Fori(0, DEPTH) as l:
                layer(l)
            for n in range(10):
                t, half = divmod(n, 2)
                m = P if t < NT else NB
                if n == 0:
                    pe.wait_ge(*x_ready(DEPTH, KD))
                if n >= 4:
                    pe.wait_ge(y_ev.sem, n - 3)
                for i in range(4):
                    last = turn(ps[0:m, n % 4, i * P:(i + 1) * P], xT[:, 4 * half + i, t * P:t * P + m], ident)
                last.then_inc(y_mm.sem, 1)

        @block.scalar
        def _(act):
            def copy(out, in_):
                return nc.scalar.activation(out, in_, ACT.Copy)

            for k in range(KD):
                act.wait_ge(x_turned.sem, k + 1)
                b = 2 * (k % 2)
                copy(xT[:, k, 0:SEQ], ps[:, b, :])
                copy(xT[:, k, SEQ:TOK], ps[:, b + 1, 0:NB]).then_inc(x_ready.sem, 1)

            def roots(l, n):
                for f in range(2):
                    act.wait_ge(*var_ready(l, 2 * n + f + 1))
                    r = rstd[:, f * HT:(f + 1) * HT]
                    nc.scalar.activation(r, r, ACT.Sqrt).then_inc(root_ready.sem, 1)

            def squares_of_x(l, n):
                for k in range(KD):
                    act.wait_ge(*x_ready(l, 4 * n + k + 1))
                    if k >= 4:
                        act.wait_ge(*sq_used(l, KD * n + k - 3))
                    nc.scalar.activation(SQ[:, k % 4, :], xT[:, k, :], ACT.Square).then_inc(sq_ready.sem, 1)

            def output_tile(l, n, g, k):
                act.wait_ge(*tile_done(l, g + 1))
                if k >= 4:
                    act.wait_ge(*sq_used(l, KD * n + k - 3))
                copy(halves(mo[:, k, :]), main(g))
                nc.scalar.activation(halves(SQ[:, k % 4, :]), main(g), ACT.Square).then_inc(evac.sem, 1)

            def layer(l):
                act.wait_ge(*prep_mm(l, 1))
                act.wait_ge(*x_ready(l, KD))
                copy(V[:, 0:124], ps[:, 7, 0:124]).then_inc(prep_ev.sem, 1)
                copy(prevs[:, :], ps[:, 7, P:P + 32]).then_inc(prep_ev.sem, 1)
                copy(conv_T[:, :, :].rearrange("p i c -> p (i c)"), ps[:, 6, 0:16 * NF]).then_inc(prep_ev.sem, 1)
                squares_of_x(l, 0)
                roots(l, 0)
                act.wait_ge(*out_sync(l, 0))
                for t in range(5):
                    m, bank = (P, t) if t < NT else (NB, 6)
                    act.wait_ge(*kv_mm(l, t + 1))
                    copy(NAT[0:m, t, :], ps[0:m, bank, 0:KVW]).then_inc(kv_ev.sem, 1)

                def q_copy(j, g):
                    act.wait_ge(*tile_done(l, g + 1))
                    if j >= 2:
                        act.wait_ge(*rot_mm(l, j - 1))
                        act.wait_ge(*qc_ready(l, j - 1))
                    copy(halves(QZ[:, j % 2, :]), main(g)).then_inc(evac.sem, 1)

                q_copy(0, QI_T)
                q_copy(1, QI_T + 1)
                act.wait_ge(*nat_ready(l, 1))
                for a in range(2):
                    ki2 = copy(kid[:, :, a, :], NAT[:, :, 128:192])
                ki2.then_inc(kid_ready.sem, 1)
                act.wait_ge(*kt_mm(l, 1))
                copy(kiT[:, 0:SEQ], ps[:, 4, :]).then_inc(kt_ev.sem, 1)
                act.wait_ge(*kt_mm(l, 2))
                copy(kT[:, 0:SEQ], ps[:, 5, :]).then_inc(kt_ev.sem, 1)
                act.wait_ge(*kt_mm(l, 3))
                copy(kiT[:, SEQ:TOK], ps[:, 7, 0:NB]).then_inc(kt_ev.sem, 1)
                copy(kT[:, SEQ:TOK], ps[:, 7, 8:8 + NB]).then_inc(kt_ev.sem, 1)
                q_copy(2, QI_T + 2)
                q_copy(3, QI_T + 3)
                for d in range(24):
                    n = P * (2 + d // 8)
                    act.wait_ge(*dot_mm(l, d + 1))
                    if d >= 4:
                        act.wait_ge(*dot_acc(l, d - 3))
                    nc.scalar.activation(RB[:, d % 4, 0:n], ps[:, 4 + d % 2, 0:n], ACT.Relu).then_inc(dot_relu.sem, 1)
                act.wait_ge(*qib_mm(l, 1))
                q = qib[:, :, :]
                heads = "p b (j two) -> p two j b"
                lo, hi = slice(0, 64), slice(64, 128)
                low = q[lo, :, 0:8].rearrange(heads, two=2)
                high = q[hi, :, 8:16].rearrange(heads, two=2)
                swapped = ps[:, 6, 0:32].rearrange("p (j b) -> p j b", j=4)
                copy(low[:, 0], qiT[lo, :, SEQ:TOK]).then_inc(qib_ev.sem, 1)
                copy(low[:, 1], swapped[lo]).then_inc(qib_ev.sem, 1)
                copy(high[:, 1], qiT[hi, :, SEQ:TOK]).then_inc(qib_ev.sem, 1)
                copy(high[:, 0], swapped[hi]).then_inc(qib_ev.sem, 1)
                act.wait_ge(*qib_mm(l, 2))
                copy(wbc[:, :, :].rearrange("p b h -> p (b h)"), ps[:, 7, 0:64]).then_inc(qib_ev.sem, 1)
                for g in range(16):
                    act.wait_ge(*pg_mm(l, g + 1))
                    if g >= 2:
                        act.wait_ge(*sdot_mm(l, g - 1))
                    copy(KIS[:, g % 2, :], ps[:, 4 + g % 2, :]).then_inc(pg_ev.sem, 1)
                for j in range(4):
                    act.wait_ge(*tile_done(l, XP_T + j + 1))
                    X = ps[:, 2 * (j % 2):2 * (j % 2) + 2, :]
                    copy(XPb[:, j, POOL_BUF:POOL_BUF + HT], X[:, 0, 0:HT])
                    copy(XPb[:, j, POOL_BUF + HT:], X[:, 1, 0:SEQ - HT])
                    copy(XS[:, j, :], X[:, 1, SEQ - HT:HT]).then_inc(evac.sem, 1)
                act.wait_ge(*sT_mm(l, 1))
                copy(S[:, 0:256].rearrange("p (r e) -> p e r", e=2),
                     ps[0:64, 4, 0:256].rearrange("p (e r) -> p e r", e=2)).then_inc(sT_ev.sem, 1)
                for j in range(4):
                    q_copy(4 + j, Q_T + j)
                act.wait_ge(*pout_mm(l, 1))
                act.wait_ge(*qc_ready(l, 8))
                copy(POUT[0:15, :], ps[0:15, 6, :])
                copy(POUT2[:, :], ps[0:NB, 7, :]).then_inc(pout_ev.sem, 1)
                for g in range(4):
                    act.wait_ge(*tile_done(l, PM_T + g + 1))
                    nc.scalar.activation(halves(hT[:, 4 + g, :]), main(g), ACT.Copy, scale=V[:, 32 + g:33 + g]
                                         ).then_inc(evac.sem, 1)
                act.wait_ge(*rope_done(l, 8))
                copy(qb[lo, :, 0:4].rearrange("p b j -> p j b"), qT[lo, :, SEQ:TOK]).then_inc(qib_ev.sem, 1)
                copy(qb[hi, :, 4:8].rearrange("p b j -> p j b"), qT[hi, :, SEQ:TOK]).then_inc(qib_ev.sem, 1)

                def exponentials(i):
                    n = P * (1 + i // N_HEADS)
                    act.wait_ge(*neg_max(l, i + 1))
                    if i >= 4:
                        act.wait_ge(*pt_mm(l, i - 3))
                    a = att[:, i % 4, :]
                    nc.scalar.activation(ARP[:, i % 4, 0:n], ARS[:, i % 2, 0:n], ACT.Exp, bias=a[:, 0:1],
                                         accum_out=a[:, 1:2]).then_inc(exp_done.sem, 1)

                def probs_copied(i):
                    n = P * (1 + i // N_HEADS)
                    act.wait_ge(*pt_mm(l, i + 1))
                    if i >= 2:
                        act.wait_ge(*pv_mm(l, i - 1))
                    copy(ART[:, i % 2, 0:n], ps[:, 4 + i % 2, 0:n]).then_inc(pt_ev.sem, 1)

                for i in range(UNITS + 3):
                    if i < UNITS:
                        exponentials(i)
                    if 2 <= i < UNITS + 2:
                        probs_copied(i - 2)
                    if i >= 3 and (i - 3) % N_HEADS == N_HEADS - 1:
                        t = (i - 3) // N_HEADS
                        act.wait_ge(*pv_mm(l, i - 2))
                        copy(hT[:, 0:4, t * P:(t + 1) * P], ps[:, 6 + t % 2, :].rearrange("p (j q) -> p j q", j=4)
                             ).then_inc(o_ev.sem, 1)
                    if i == 12:
                        act.wait_ge(*list_mm(l, 1))
                        copy(ix[:, :, :, :], ps[0:16, 3, 256:512].rearrange("p (b w i) -> p w b i", w=2, i=16)
                             ).then_inc(list_ev.sem, 1)
                for q in range(4):
                    act.wait_ge(*ks_mm(l, q + 1))
                    copy(KTS[:, 4 * q:4 * q + 4, :].rearrange("p j d -> p (j d)"), ps[:, 3, :]).then_inc(ks_ev.sem, 1)
                act.wait_ge(*qs_mm(l, 1))
                copy(sc2[:, :], ps[:, 3, 0:P]).then_inc(qs_ev.sem, 1)
                act.wait_ge(*qs_mm(l, 3))
                copy(SA[:, 0:256], ps[0:64, 3, P:3 * P]).then_inc(qs_ev.sem, 1)
                act.wait_ge(*ss_ready(l, 1))
                nc.scalar.activation(PA[:, :], SA[:, :], ACT.Exp, bias=sm[:, 0:1], accum_out=sm[:, 1:2]
                                     ).then_inc(se_ready.sem, 1)
                act.wait_ge(*sp_mm(l, 1))
                copy(pT2[:, :, :].rearrange("p t c -> p (t c)"), ps[:, 3, 0:P]).then_inc(sp_ev.sem, 1)
                copy(pn[:, :], ps[0:8, 3, P:P + 64]).then_inc(sp_ev.sem, 1)
                act.wait_ge(*so_mm(l, 1))
                for n in range(2):
                    r = slice(64 * n, 64 * n + 64)
                    o = ps[r, 3, 256:320].rearrange("p (b h) -> p h b", b=NB)
                    copy(hT[r, 0:4, SEQ:TOK], o[:, 4 * n:4 * n + 4, :]).then_inc(so_ev.sem, 1)

                for m in range(KD):
                    output_tile(l, 1, WO_T + m, m)
                roots(l, 1)
                squares_of_x(l, 2)
                roots(l, 2)

                def gate_tile(i, u, first):
                    act.wait_ge(*tile_done(l, i * 2 + GV_T + 1))
                    if not first:
                        act.wait_ge(*conv_done(l, i - 1))
                        act.wait_ge(*co_mm(l, i - 1))
                    copy(halves(G[:, u, 2:522]), main(0)).then_inc(evac.sem, 1)
                    act.wait_ge(*conv_done(l, i + 1))
                    if not first:
                        act.wait_ge(*val_used(l, i - 1))
                    nc.scalar.activation(GE[:, u, :], CV[:, u, :], ACT.Gelu_apprx_tanh).then_inc(gelu_done.sem, 1)
                    act.wait_ge(*co_mm(l, i + 1))
                    out = CVO[:, :].rearrange("p (i n) -> p i n", n=P)
                    copy(out[:, i:i + 1, :] if isinstance(i, int) else out[:, bass.ds(i, 1), :],
                         ps[0:10, 6 + u, 0:P].rearrange("p (a n) -> p a n", a=1)).then_inc(co_ev.sem, 1)

                for u in range(2):
                    gate_tile(u, u, True)
                with act.Fori(1, NF // 2) as r:
                    for u in range(2):
                        gate_tile(r * 2 + u, u, False)
                for m in range(KD):
                    output_tile(l, 3, DN_T + m, m)
                roots(l, 3)

            with act.Fori(0, DEPTH) as l:
                layer(l)
            for n in range(10):
                t, half = divmod(n, 2)
                act.wait_ge(y_mm.sem, n + 1)
                dst = x_rows[:, t, :] if t < NT else xs_rows
                m = P if t < NT else NB
                copy(dst[0:m, 512 * half:512 * half + 512], ps[0:m, n % 4, :]).then_inc(y_ev.sem, 1)

        @block.vector
        def _(dve):
            tt, ts, stt = nc.vector.tensor_tensor, nc.vector.tensor_scalar, nc.vector.scalar_tensor_tensor

            nc.vector.memset(NAT[:, :, :], 0.0)
            nc.vector.memset(XPb[:, :, 0:POOL_BUF], 0.0)
            nc.vector.memset(qib[:, :, :], 0.0)
            nc.vector.memset(qb[:, :, :], 0.0)
            nc.vector.memset(base[:, :], 0.0)
            dve.wait_ge(const_in.sem, 32)
            for g in range(2):
                r = slice(64 * g, 64 * g + 64)
                ts(idxI[r, :, :], PT[r, :, g:NPG:2], 64.0, const("row64")[r], ALU.mult, ALU.add
                   ).then_inc(tables.sem, 1)
            nc.vector.tensor_copy(phys[:, :, :, :], PT[:, :, :].rearrange("p b (j two) -> p two b j", two=2)
                                  ).then_inc(tables.sem, 1)

            def inverse_root(l, n):
                dve.wait_ge(*sq_used(l, KD * (n + 1)))
                for f in range(2):
                    ts(rstd[:, f * HT:(f + 1) * HT], ps[:, 4 + f, 0:HT], 1.0 / D_MODEL, EPS, ALU.mult, ALU.add
                       ).then_inc(var_ready.sem, 1)
                for f in range(2):
                    r = rstd[:, f * HT:(f + 1) * HT]
                    dve.wait_ge(*root_ready(l, 2 * n + f + 1))
                    nc.vector.reciprocal(r, r).then_inc(rstd_ready.sem, 1)
                dve.wait_ge(*rstd_ready(l, 2 * n + 2))

            def normed(l, n, a):
                inverse_root(l, n)
                for k in range(KD):
                    stt(hT[:, k, :], xT[:, k, :], gain(a, k), rstd[:, :], ALU.mult, ALU.mult).then_inc(h_ready.sem, 1)

            def update(l, n, a):
                inverse_root(l, n)
                for k in range(KD):
                    stt(mo[:, k, :], mo[:, k, :], gain(a, k), rstd[:, :], ALU.mult, ALU.mult).then_inc(upd.sem, 1)

            def layer(l):
                st = dve_step
                st.begin(l)

                def then_wait(ins):
                    st.add(ins)
                    wait_alone(dve, *st.last())

                dve.wait_ge(*prep_ev(l, 3))
                normed(l, 0, G_PRE_MIX)

                dve.wait_ge(*kv_ev(l, 5))
                heads = NAT[:, :, 0:192].rearrange("p t (h d) -> p t h d", h=3)
                x1, x2 = heads[:, :, :, 0:8], heads[:, :, :, 8:16]
                c, s = (const(n).rearrange("p (t i) -> p t i", t=5).unsqueeze(2).broadcast_to([P, 5, 3, 8])
                        for n in ("cosN", "sinN"))
                r4 = [TS[:, 120 * i:120 * i + 120].rearrange("p (t h i) -> p t h i", t=5, h=3) for i in range(4)]
                st.add(tt(r4[0], x1, c, ALU.mult))
                st.add(tt(r4[1], x2, s, ALU.mult))
                st.add(tt(r4[2], x2, c, ALU.mult))
                then_wait(tt(r4[3], x1, s, ALU.mult))
                tt(x1, r4[0], r4[1], ALU.subtract)
                tt(x2, r4[2], r4[3], ALU.add).then_inc(nat_ready.sem, 1)
                ts(WI[:, :, :], NAT[:, :, 192:200], 8 ** -0.5, None, ALU.mult).then_inc(nat_ready.sem, 1)
                dve.wait_ge(*nat_ready(l, 2))
                tt(wdiag[:, :, :], WI[0:8, 4, :].unsqueeze(1).broadcast_to([8, NB, 8]),
                   ident[0:8, 0:8].unsqueeze(2).broadcast_to([8, NB, 8]), ALU.mult).then_inc(wd_ready.sem, 1)

                def rope(j):
                    dst = qiT[:, j, :] if j < 4 else qT[:, j - 4, :]
                    dve.wait_ge(*rot_mm(l, j + 1))
                    if j:
                        dve.wait_ge(*rope_done(l, j))
                    tt(halves(TS[:, :]), ps[:, 6:8, 0:HT], halves(const("sinT")), ALU.mult).then_inc(rot_used.sem, 1)
                    dve.wait_ge(*rot_used(l, j + 1))
                    dve.wait_ge(*qc_ready(l, j + 1))
                    tt(dst, TS[:, :], QC[:, j % 2, :], ALU.add).then_inc(rope_done.sem, 1)

                for j in range(4):
                    rope(j)
                for d in range(24):
                    t, h = 1 + d // 8, d % 8
                    n = P * (t + 1)
                    sc = SCT[:, KEYS_BEFORE[t]:KEYS_BEFORE[t] + n]
                    dve.wait_ge(*dot_relu(l, d + 1))
                    if h:
                        dve.wait_ge(*dot_acc(l, d))
                    stt(sc, RB[:, d % 4, 0:n], WI[:, t, h:h + 1],
                        sc if h else const("mask")[:, 384 - P * t:384 - P * t + n],
                        ALU.mult, ALU.add).then_inc(dot_acc.sem, 1)
                wait_alone(dve, *dot_acc(l, 24))

                def choose(t, r):
                    lo, n = KEYS_BEFORE[t], P * (t + 1)
                    left = (SCT if r == 0 else WK)[:, lo:lo + n]
                    then_wait(nc.vector.max(M8[:, :], left))
                    then_wait(nc.vector.match_replace(WK[:, lo:lo + n], M8[:, :], left, TAKEN))
                    if r == TOPK_P // 8 - 1:
                        tt(NOT[:, lo:lo + n], WK[:, lo:lo + n], SCT[:, lo:lo + n], ALU.is_ge
                           ).then_inc(sel_ready.sem, 1)

                for t in (1, 2):
                    for r in range(TOPK_P // 8):
                        choose(t, r)

                dve.wait_ge(*sdot_mm(l, 17))
                dve.wait_ge(*qib_ev(l, 5))
                for b in range(NB):
                    stt(SW[:, P * b:P * b + P].rearrange("p (j h) -> p j h", h=8),
                        ps[:, 6 + b // 4, P * (b % 4):P * (b % 4) + P].rearrange("p (j h) -> p j h", h=8), 0.0,
                        wbc[:, b:b + 1, :].broadcast_to([P, 16, 8]), ALU.max, ALU.mult).then_inc(sw_used.sem, 1)
                stt(sdot[:, :], ps[0:8, 4, 0:64], 0.0, wdiag[:, :, :].rearrange("p b h -> p (b h)"),
                    ALU.max, ALU.mult).then_inc(sw_used.sem, 1)
                dve.wait_ge(*sw_used(l, 9))
                nc.vector.tensor_reduce(sTok[:, :], SW.rearrange("p (c h) -> p c h", h=8), AX.X, ALU.add
                                        ).then_inc(stok_ready.sem, 1)
                nc.vector.tensor_reduce(snew[:, :], sdot[:, :], AX.X, ALU.add).then_inc(stok_ready.sem, 1)

                cand = candI[:, 0:1].bitcast(F32)
                thr = cols[:, 7:8]

                def count(s):
                    src, by = (S, 0.0) if s == 0 else (S2, cand)
                    ts(J[:, :], src[:, :], by, None, ALU.is_ge, ALU.add, accum_out=(cntB if s % 2 else cntA)
                       ).then_inc(cnt_ready.sem, 1)

                def counted(s):
                    return ps[0:64, 4 + s % 2, 300:301]

                def bits_start():
                    dve.wait_ge(*sT_ev(l, 1))
                    dve.wait_ge(*sT_mm(l, 2))
                    then_wait(tt(S[:, 256:257], ps[0:64, 5, 0:1], const("newneg", 64), ALU.add))
                    count(0)

                def bits_sign():
                    dve.wait_ge(*cnt_mm(l, 1))
                    then_wait(ts(cols[:, 8:9], counted(0), float(TOPK_S), -2.0, ALU.is_lt, ALU.mult))
                    st.add(ts(sgn, cols[:, 8:9], 1.0, None, ALU.add))
                    then_wait(ts(kth, cols[:, 8:9], -(PAST + 1 - 2 * TOPK_S + 1) / 2.0, float(TOPK_S),
                                 ALU.mult, ALU.add))
                    st.add(ts(S2[:, 0:256], S[:, 0:256], sgn, None, ALU.mult))
                    st.add(stt(S2[:, 256:257], ps[0:64, 5, 0:1], sgn, const("newneg", 64), ALU.mult, ALU.add))
                    then_wait(nc.vector.tensor_copy(candI[:, 0:1], const("bits", 64).bitcast(I32)[:, 30:31]))
                    count(1)

                def bit(s):
                    b = BITS - s
                    bits = const("bits", 64).bitcast(I32)
                    dve.wait_ge(*cnt_mm(l, s + 1))
                    then_wait(ts(candI[:, 1:2], counted(s), kth, float(1 << b), ALU.is_lt, ALU.mult))
                    if b:
                        then_wait(stt(candI[:, 0:1], candI[:, 1:2], bits[:, b - 1:b], candI[:, 0:1],
                                      ALU.bitwise_or, ALU.bitwise_xor))
                        count(s + 1)
                    else:
                        then_wait(tt(candI[:, 0:1], candI[:, 1:2], candI[:, 0:1], ALU.bitwise_xor))
                        then_wait(tt(thr, cand, sgn, ALU.mult))

                steps = [bits_start, bits_sign] + [lambda s=s: bit(s) for s in range(1, BITS + 1)]

                def pooled(g):
                    w = WINDOWS[g]
                    res = (LA[:, 0], LB[:, 0], LA[:, 2], LB[:, 2])[g]
                    edge = const("edge")[:, POOL_BUF * g:POOL_BUF * (g + 1)]
                    if g == 0:
                        dve.wait_ge(*sums_ready(l, 4))
                        dve.wait_ge(*evac(l, Q_T))
                    then_wait(tt(res[:, 15:30], res[:, 15:30], edge, ALU.mult))
                    stt(DIFF[:, g, 0:SEQ], res[:, 15:527], 1.0 / w, XPb[:, g, 15:527], ALU.mult, ALU.subtract
                        ).then_inc(diff_ready.sem, 1)
                    stt(DIFF[:, g, SEQ:TOK], XS[:, g, :], 1.0 / w - 1.0, prevs[:, 8 * g:8 * g + 8],
                        ALU.mult, ALU.add).then_inc(diff_ready.sem, 1)

                for r in range(TOPK_P // 8):
                    choose(3, r)
                    for _ in range(2):
                        if steps:
                            steps.pop(0)()
                    for j in {4: (4,), 6: (5,), 7: (6, 7)}.get(r, ()):
                        rope(j)
                    if r == 7:
                        for g in range(4):
                            pooled(g)
                while steps:
                    steps.pop(0)()

                def pick_a():
                    ts(J[:, :], S[:, :], thr, None, ALU.is_gt, ALU.add, accum_out=cntA).then_inc(pick_ready.sem, 1)
                    ts(J2[:, :], S[:, :], thr, None, ALU.is_equal, ALU.add, accum_out=cntB
                       ).then_inc(pick_ready.sem, 1)

                def pick_b():
                    dve.wait_ge(*pick_mm(l, 2))
                    dve.wait_ge(*pick_ready(l, 2))
                    st.add(ts(need, ps[0:64, 3, 0:1], -1.0, float(TOPK_S), ALU.mult, ALU.add))
                    then_wait(nc.vector.tensor_copy(offs, ps[0:64, 3, 1:2]))
                    then_wait(nc.vector.tensor_tensor_scan(S2[:, :], J2[:, :], J2[:, :], offs, ALU.add, ALU.bypass))
                    then_wait(stt(S2[:, :], S2[:, :], need, J2[:, :], ALU.is_le, ALU.mult))
                    then_wait(tt(J[:, :], J[:, :], S2[:, :], ALU.add))
                    ts(J2[:, 0:256], J[:, 0:256], 1.0, None, ALU.mult, ALU.add, accum_out=cntA
                       ).then_inc(pick_ready.sem, 1)

                def pick_c():
                    dve.wait_ge(*pick_mm(l, 4))
                    st.add(nc.vector.tensor_copy(snegc, ps[0:64, 3, 3:4]))
                    then_wait(nc.vector.tensor_copy(offs, ps[0:64, 3, 2:3]))
                    then_wait(nc.vector.tensor_tensor_scan(S2[:, 0:256], J[:, 0:256], J[:, 0:256], offs,
                                                           ALU.add, ALU.bypass))
                    tt(S2[:, 0:256], S2[:, 0:256], J[:, 0:256], ALU.mult).then_inc(pick_ready.sem, 1)

                def pick_d():
                    dve.wait_ge(*pos_mm(l, 1))
                    then_wait(ts(posI[:, 0, :], ps[:, 3, P:2 * P], -1.0, None, ALU.add))
                    st.add(ts(posI[:, 1, :], posI[:, 0, :], 4, None, ALU.arith_shift_right))
                    then_wait(ts(posI[:, 2, :], posI[:, 0, :], 15, None, ALU.bitwise_and))
                    iota = const("iota16").unsqueeze(1).broadcast_to([P, P, 16])

                    def wide(ap):
                        return ap.unsqueeze(2).broadcast_to([P, P, 16])
                    st.add(tt(OA[:, :, :], wide(posI[:, 1, :]), iota, ALU.is_equal))
                    then_wait(tt(OB[:, :, 1, :], wide(posI[:, 2, :]), iota, ALU.is_equal))
                    then_wait(tt(OB[:, :, 0, :], OB[:, :, 1, :], wide(phys[:, :, :, :].rearrange("p g b j -> p (g b j)")),
                                 ALU.mult))
                    ts(OB[:, :, 1, :], OB[:, :, 1, :], const("tok"), None, ALU.mult).then_inc(hot_ready.sem, 1)

                def pick_e():
                    dve.wait_ge(*list_ev(l, 1))
                    then_wait(stt(ixf[:, :, :], ix[:, 0], float(PAGE), ix[:, 1], ALU.mult, ALU.add))
                    ts(ixi[:, :, :], ixf[:, :, :], base[0:16, :], None, ALU.add).then_inc(list_ready.sem, 1)

                picks = {0: pick_a, 2: pick_b, 4: pick_c, 6: pick_d, 14: pick_e}

                def masked(i):
                    t = i // N_HEADS
                    n = P * (t + 1)
                    dve.wait_ge(*qk_mm(l, i + 1))
                    if i >= 2:
                        dve.wait_ge(*exp_done(l, i - 1))
                    if t == 0:
                        tt(ARS[:, i % 2, 0:n], ps[:, i % 3, 0:n], const("mask")[:, 384:512], ALU.add
                           ).then_inc(qk_used.sem, 1)
                    else:
                        stt(ARS[:, i % 2, 0:n], NOT[:, KEYS_BEFORE[t]:KEYS_BEFORE[t] + n], NEG, ps[:, i % 3, 0:n],
                            ALU.mult, ALU.add).then_inc(qk_used.sem, 1)
                    dve.wait_ge(*qk_used(l, i + 1))
                    nc.vector.tensor_reduce(att[:, i % 4, 0:1], ARS[:, i % 2, 0:n], AX.X, ALU.max, negate=True
                                            ).then_inc(neg_max.sem, 1)

                def normalised(i):
                    n = P * (1 + i // N_HEADS)
                    dve.wait_ge(*exp_done(l, i + 1))
                    then_wait(nc.vector.reciprocal(att[:, i % 4, 2:3], att[:, i % 4, 1:2]))
                    ts(ARP[:, i % 4, 0:n], ARP[:, i % 4, 0:n], att[:, i % 4, 2:3], None, ALU.mult
                       ).then_inc(prob_ready.sem, 1)

                dve.wait_ge(*sel_ready(l, 3))
                for i in range(UNITS + 1):
                    if i < UNITS:
                        masked(i)
                    if i in picks:
                        picks[i]()
                    if i >= 1:
                        normalised(i - 1)

                dve.wait_ge(*qs_mm(l, 3))
                dve.wait_ge(*qs_ev(l, 2))
                then_wait(tt(tmp8[:, :], ps[0:64, 3, 400:408], const("diag", 64), ALU.mult))
                then_wait(nc.vector.tensor_reduce(SA[:, 256:257], tmp8[:, :], AX.X, ALU.add))
                then_wait(ts(cols[:, 9:10], snegc, -NEG, NEG, ALU.mult, ALU.add))
                st.add(tt(SA[:, 256:257], SA[:, 256:257], cols[:, 9:10], ALU.add))
                then_wait(stt(SA[:, 255:256], snegc, NEG, SA[:, 255:256], ALU.mult, ALU.add))
                nc.vector.tensor_reduce(sm[:, 0:1], SA[:, :], AX.X, ALU.max, negate=True).then_inc(ss_ready.sem, 1)
                dve.wait_ge(*se_ready(l, 1))
                then_wait(nc.vector.reciprocal(sm[:, 2:3], sm[:, 1:2]))
                ts(PA[:, :], PA[:, :], sm[:, 2:3], None, ALU.mult).then_inc(sp_ready.sem, 1)
                dve.wait_ge(*sp_ready(l, 1))
                ts(pnd[:, :], const("diag", 64), PA[:, 256:257], None, ALU.mult).then_inc(sp_ready.sem, 1)
                st.add(ts(base[:, :], base[:, :], float(N_PHYS * PAGE), None, ALU.add))

                update(l, 1, G_POST_MIX)
                normed(l, 2, G_PRE_FFN)

                for u in range(2):
                    ms = nc.vector.memset(G[:, u, 0:2], 0.0)
                then_wait(ms)
                st.end()

                def conv_tile(i, u, rnd, first):
                    fs = ffn_step
                    fs.begin(rnd * 2 + u)
                    col = (lambda at: V[:, at + i:at + i + 1]) if isinstance(i, int) else \
                        (lambda at: V[:, bass.ds(i + at, 1)])
                    w0, w1, w2, bias = (col(a) for a in (36, 36 + NF, 36 + 2 * NF, 102))
                    cs = conv_T[:, i:i + 1, :] if isinstance(i, int) else conv_T[:, bass.ds(i, 1), :]
                    cs = cs.rearrange("p a (b j) -> p (a b) j", j=2)
                    g, cv = G[:, u, :], CV[:, u, :]
                    dve.wait_ge(*evac(l, i + (EVAC_GATE + 1)))
                    if not first:
                        dve.wait_ge(*gelu_done(l, i - 1))
                    fs.add(ts(cv[:, 0:SEQ], g[:, 0:SEQ], w0, bias, ALU.mult, ALU.add))
                    fs.add(ts(cv[:, SEQ:TOK], cs[:, :, 0], w0, bias, ALU.mult, ALU.add))
                    dve.wait_ge(*fs.last())
                    fs.add(stt(cv[:, 0:SEQ], g[:, 1:SEQ + 1], w1, cv[:, 0:SEQ], ALU.mult, ALU.add))
                    fs.add(stt(cv[:, SEQ:TOK], cs[:, :, 1], w1, cv[:, SEQ:TOK], ALU.mult, ALU.add))
                    dve.wait_ge(*fs.last())
                    stt(cv[:, :], g[:, 2:TOK + 2], w2, cv[:, :], ALU.mult, ALU.add).then_inc(conv_done.sem, 1)
                    fs.end()
                    dve.wait_ge(*gelu_done(l, i + 1))
                    dve.wait_ge(*tile_done(l, i * 2 + (GV_T + 2)))
                    y = yT[:, i:i + 1, :] if isinstance(i, int) else yT[:, bass.ds(i, 1), :]
                    tt(y.rearrange("p a (f t) -> p (a f) t", f=2), halves(GE[:, u, :]), main(1), ALU.mult
                       ).then_inc(val_used.sem, 1)

                for u in range(2):
                    conv_tile(u, u, l * (NF // 2), True)
                with dve.Fori(1, NF // 2) as r:
                    for u in range(2):
                        conv_tile(r * 2 + u, u, l * (NF // 2) + r, False)

                update(l, 3, G_POST_FFN)

            with dve.Fori(0, DEPTH) as l:
                layer(l)


_SHAPES = {
    "y_prompt": (1, SEQ, D_MODEL), "y_sample": (NB, 1, D_MODEL),
    "new_k_prompt": (DEPTH, 1, SEQ, 2, HD), "new_v_prompt": (DEPTH, 1, SEQ, 2, HD),
    "new_ik_prompt": (DEPTH, 1, SEQ, HD), "new_pool_prompt": (DEPTH, 1, POOL_BUF, 512),
    "new_conv_prompt": (DEPTH, 1, 2, D_FF),
    "new_k_sample": (DEPTH, NB, 1, 2, HD), "new_v_sample": (DEPTH, NB, 1, 2, HD),
    "new_ik_sample": (DEPTH, NB, 1, HD), "new_pool_sample": (DEPTH, NB, POOL_BUF, 512),
    "new_conv_sample": (DEPTH, NB, 2, D_FF),
}


def kernel(**inputs):
    import concourse.bacc as bacc
    from concourse.bass_utils import run_bass_kernel_spmd

    nc = bacc.Bacc("TRN2", target_bir_lowering=False, num_devices=1)
    arrays = {f"in_{n}": np.ascontiguousarray(a) for n, a in inputs.items()}
    arrays["in_consts"] = constants()
    A = {n[3:]: nc.dram_tensor(n, a.shape, mybir.dt.from_np(a.dtype), kind="ExternalInput").ap()
         for n, a in arrays.items()}
    O = {n: nc.dram_tensor(f"out_{n}", s, F32, kind="ExternalOutput").ap() for n, s in _SHAPES.items()}
    scratch = nc.dram_tensor("slot_lists", (NB, TOPK_S), I32, kind="Internal").ap()
    build(nc, A, O, scratch)
    r = run_bass_kernel_spmd(nc, [arrays], core_ids=[0])
    return tuple(r.results[0][f"out_{n}"] for n in _SHAPES)
```

```python
from contextlib import ExitStack

import numpy as np

import concourse.bass as bass
from concourse import mybir

F32 = mybir.dt.float32
BF16 = mybir.dt.bfloat16
F32R = mybir.dt.float32r
I32 = mybir.dt.int32
ALU = mybir.AluOpType
ACT = mybir.ActivationFunctionType
AX = mybir.AxisListType

P = 128
D_MODEL, SEQ, DEPTH, NB = 1024, 512, 2, 8
PAST, PAGE = 2048, 128
N_PHYS = 160
N_HEADS, HD = 8, 64
TOPK_P, TOPK_S = 128, 256
WINDOWS = (2, 4, 8, 16)
POOL_BUF = 15
D_FF = 2816
EPS = 1e-6
ROPE_THETA = 500000.0
Q0, K0, V0, QI0, KI0, XP0, IN_WIDTH = 0, 512, 640, 768, 1280, 1352, 1864

KD = D_MODEL // P
NF = D_FF // P
TOK = SEQ + NB
HT = TOK // 2
NT = SEQ // P
NPG = PAST // PAGE
NPP = NPG // 2
KVW = 328
NEG = -3.0e38
TAKEN = -3.3e38
KEYS_BEFORE = {1: 0, 2: 256, 3: 640}
KEYS_ALL = 1152

_CONST = [("ident", P), ("ones", P), ("cosT", TOK), ("sinT", TOK), ("cosN", 40), ("sinN", 40), ("rot", P),
          ("swap", P), ("mask", 896), ("same", 64), ("below", 64), ("newneg", 1), ("newrow", 64),
          ("newto", 64), ("diag", 8), ("iota16", 16), ("tok", 1), ("row64", 1), ("edge", 60), ("wsel", 32),
          ("bits", 32)]
CO, _n = {}, 0
for _name, _w in _CONST:
    CO[_name] = (_n, _n + _w)
    _n += _w
NCONST = _n


def constants():
    c = np.zeros((P, NCONST), np.float32)

    def put(name, a, rows=P):
        lo, hi = CO[name]
        c[:rows, lo:hi] = a

    put("ident", np.eye(P))
    put("ones", 1.0)
    pos = np.concatenate([np.arange(SEQ), np.full(NB, PAST)]).astype(np.float32)
    half = 8
    inv = (np.float32(ROPE_THETA) ** (-np.arange(half, dtype=np.float32) / np.float32(half))).astype(np.float32)
    ang = (pos[:, None] * inv[None, :]).astype(np.float32).astype(np.float64)
    cos, sin = np.cos(ang), np.sin(ang)
    ct, st, rot = np.ones((P, TOK)), np.zeros((P, TOK)), np.zeros((P, P))
    for p in range(P):
        d = p % HD
        if d < half:
            ct[p], st[p], rot[p + half, p] = cos[:, d], -sin[:, d], 1.0
        elif d < 2 * half:
            ct[p], st[p], rot[p - half, p] = cos[:, d - half], sin[:, d - half], 1.0
    put("cosT", ct * HD ** -0.5)
    put("sinT", st * HD ** -0.5)
    put("rot", rot)
    cn, sn = np.ones((P, 5, half)), np.zeros((P, 5, half))
    for t in range(5):
        rows = P if t < 4 else NB
        cn[:rows, t], sn[:rows, t] = cos[t * P:t * P + rows], sin[t * P:t * P + rows]
    put("cosN", cn.reshape(P, 40))
    put("sinN", sn.reshape(P, 40))
    put("swap", np.eye(P)[(np.arange(P) + 64) % P])
    p, q = np.arange(P)[:, None], np.arange(896)[None, :]
    put("mask", np.where(q <= p + 384, 0.0, NEG))
    r, m = np.arange(64)[:, None], np.arange(64)[None, :]
    put("same", (r // 8 == m // 8), 64)
    put("below", (r // 8 == m // 8) & (r < m), 64)
    put("newneg", np.where(r % 8 == 7, 0.0, NEG), 64)
    b8 = np.arange(8)[:, None]
    put("newrow", (m == 8 * b8 + 7), 8)
    put("newto", (r % 8 == 7) & (r // 8 == m // 8), 64)
    put("diag", (r // 8 == np.arange(8)[None, :]), 64)
    put("iota16", np.arange(16)[None, :])
    put("tok", np.arange(P)[:, None])
    put("row64", np.arange(P)[:, None] % 64)
    put("edge", np.array([[w / min(t + 1, w) for t in range(POOL_BUF)] for w in WINDOWS]).reshape(1, 60))
    ws = np.zeros((P, 4, 8))
    for b in range(NB):
        for g, w in enumerate(WINDOWS):
            ws[b * POOL_BUF + POOL_BUF - (w - 1):(b + 1) * POOL_BUF, g, b] = 1.0 / w
    put("wsel", ws.reshape(P, 32))
    lo, hi = CO["bits"]
    c.view(np.int32)[:, lo:hi] = 0
    for b in range(31):
        c.view(np.int32)[:, lo + b] = 1 << b
    return c


QI_T, XP_T, Q_T, PM_T, WO_T, GV_T = 0, 4, 8, 12, 16, 24
DN_T = GV_T + 2 * NF
TILES = DN_T + KD
EVAC_DN = GV_T
EVACS = EVAC_DN + KD
C_WO, C_GV = 8, 12
C_DN = C_GV + NF
CHUNKS = C_DN + KD
CHUNK_DMAS = {0: 3, 1: 1, 2: 1, 3: 1, 4: 1, 5: 4, 6: 4, 7: 1, 8: 3, 9: 3, 10: 3, 11: 3}


def dmas_before(c):
    return sum(CHUNK_DMAS.get(i, 1) for i in range(c % 2, c + 1, 2))


SLOT_DMAS = (dmas_before(CHUNKS - 2), dmas_before(CHUNKS - 1))
UNITS = NT * N_HEADS
BITS = 31
EARLY_ROUNDS = 13
SPLITS = 2 * NF + 2 * KD


def build(nc, A, O, scratch):
    ctx = ExitStack()

    class Signal:

        def __init__(self, name, per, first=0):
            self.sem, self.per, self.first = ctx.enter_context(nc.semaphore(name)), per, first

        def __call__(self, rnd, n):
            return self.sem, rnd * self.per + (n + self.first)

    class Steps(Signal):

        def begin(self, rnd):
            self.rnd, self.n = rnd, 0

        def add(self, ins):
            ins.then_inc(self.sem, 1)
            self.n += 1

        def last(self):
            return self(self.rnd, self.n)

        def end(self):
            assert self.n == self.per, (self.sem, self.n)

    with ctx:
        place = {}

        def sb(name, shape, dt=F32):
            place[name] = -(-nc.sbuf_base // 32) * 32
            return ctx.enter_context(nc.sbuf_tensor(name, shape, dt))

        def rounded(name, shape):
            return nc.alloc_sbuf_tensor_at(name + "_r", shape, F32R, offset=place[name])

        C = sb("C", [P, NCONST])

        def const(name, rows=P):
            lo, hi = CO[name]
            return C[0:rows, lo:hi]

        ident, ones = const("ident"), const("ones")
        xT = sb("xT", [P, KD, TOK])
        hT = sb("hT", [P, KD, TOK])
        moR = sb("moR", [P, KD * TOK])
        mo = moR[:, :].rearrange("p (k t) -> p k t", k=KD)
        yR = sb("yR", [P, NF * TOK])
        yT = yR[:, :].rearrange("p (k t) -> p k t", k=NF)
        W = sb("W", [P, 2, NF * P])
        vec_rows = sb("vec_rows", [P, P])
        V = sb("V", [P, P])
        state_rows = sb("state_rows", [P, 512])
        prevs = sb("prevs", [P, 32])
        conv_T = sb("conv_T", [P, NF, 16])
        NAT = sb("NAT", [P, 5, KVW])
        kid = sb("kid", [P, 5, 2, HD])
        kT = sb("kT", [P, TOK])
        kiT = sb("kiT", [P, TOK])
        WI = sb("WI", [P, 5, 8])
        QQ = sb("QQ", [P, 8 * TOK])
        qiT = QQ[:, 0:4 * TOK].rearrange("p (k t) -> p k t", k=4)
        qT = QQ[:, 4 * TOK:].rearrange("p (k t) -> p k t", k=4)
        conv_rows = QQ[0:16, 0:D_FF]
        QZC = sb("QZC", [P, 4 * TOK])
        QZ, QC = (QZC[:, a:a + 2 * TOK].rearrange("p (a t) -> p a t", a=2) for a in (0, 2 * TOK))
        SQ = sb("SQ", [P, 4, TOK])
        RB = SQ[:, :, 0:SEQ]
        SQ0 = SQ[:, 0, :]
        ix = SQ0[0:16, 0:256].rearrange("p (w b i) -> p w b i", w=2, b=NB)
        ixf = SQ0[0:16, 256:384].rearrange("p (b i) -> p b i", b=NB)
        ixi = SQ0[0:16, 384:512].bitcast(I32).rearrange("p (b i) -> p b i", b=NB)
        sc2 = SQ[:, 1, 0:P]
        pT2 = SQ[:, 1, P:2 * P].rearrange("p (t c) -> p t c", t=2)
        TS = sb("TS", [P, TOK])
        rstd = sb("rstd", [P, TOK])
        rcol = sb("rcol", [P, 5])
        gpm = sb("gpm", [P, KD])
        SUM = TS
        SEL = sb("SEL", [P, 3 * KEYS_ALL])
        SCT, WK, NOT = (SEL[:, i * KEYS_ALL:(i + 1) * KEYS_ALL] for i in range(3))
        M8 = sb("M8", [P, 3, 8])
        XPb = sb("XPb", [P, 4, POOL_BUF + SEQ])
        XS = sb("XS", [P, 4, NB])
        G = SEL[:, 0:2 * 522].rearrange("p (a t) -> p a t", a=2)
        CV = SEL[:, 1044:1044 + 2 * TOK].rearrange("p (a t) -> p a t", a=2)
        GE = SEL[:, 2084:2084 + 2 * TOK].rearrange("p (a t) -> p a t", a=2)
        CVO = QQ[32:42, 0:D_FF]
        flat = {n: rounded(n, [P, size]) for n, size in
                (("W", 2 * NF * P), ("hT", KD * TOK), ("moR", KD * TOK), ("yR", NF * TOK), ("QZC", 4 * TOK),
                 ("SQ", 4 * TOK), ("XPb", 4 * (POOL_BUF + SEQ)), ("QQ", 8 * TOK), ("SEL", 3 * KEYS_ALL),
                 ("NAT", 5 * KVW), ("kid", 10 * HD), ("kT", TOK), ("kiT", TOK))}

        def tile_of(name, a):
            return flat[name][:, a * TOK:(a + 1) * TOK]

        def lower_w(slot, a, b):
            return flat["W"][:, slot * NF * P + a:slot * NF * P + b]
        WH = [flat["QZC"], flat["SQ"]]
        DH = [[[(0, flat["QZC"][:, 0:16 * P], 16)], [(16, flat["QQ"][:, D_FF:D_FF + 6 * P], 6)]],
              [[(0, flat["XPb"][:, 0:16 * P], 16)],
               [(16, flat["QQ"][:, D_FF + 6 * P:D_FF + 10 * P], 4), (20, flat["SEL"][:, 6 * TOK:6 * TOK + 2 * P], 2)]]]
        MIX_ORDER = (4, 5, 6, 7, 0, 1, 2, 3)
        MH = [flat["yR"][:, a:a + TOK] for a in
              [k * TOK for k in range(3)] + [4096] + [8192 + k * TOK for k in range(4)]]
        OH = [flat["QZC"][:, 0:2048], flat["yR"][:, 2048:4096]]
        YH = [tile_of(n, a) for n, tiles in (("NAT", range(3)), ("kid", range(1)), ("kT", range(1)), ("kiT", range(1)),
                                             ("SEL", range(6)), ("hT", range(8)), ("SQ", range(2, 4))) for a in tiles]
        POUT, POUT2 = QZ[0:15, 0, 0:512], QZ[0:NB, 1, 0:512]
        S, S2, J, J2, SA, PA = (yR[0:64, 6144 + 257 * i:6401 + 257 * i] for i in range(6))
        posI = yR[:, 7686:8070].bitcast(I32).rearrange("p (a c) -> p a c", a=3)
        IK = yR[:, 0:64 * P].rearrange("p (j d) -> p j d", j=64)
        KG = yR[:, 0:16 * P].rearrange("p (j d) -> p j d", j=16)
        VG = yR[:, 2048:4096].rearrange("p (j d) -> p j d", j=16)
        KTS = yR[:, 4096:6144].rearrange("p (j d) -> p j d", j=16)
        DIFF = yR[:, 8192:8192 + 4 * TOK].rearrange("p (g t) -> p g t", g=4)
        cosR, sinR = (yR[:, a:a + TOK] for a in (10272, 10272 + TOK))
        OA = yR[:, 8192:9216].bitcast(BF16).rearrange("p (c i) -> p c i", i=16)
        OB = yR[:, 9216:11264].bitcast(BF16).rearrange("p (c w i) -> p c w i", w=2, i=16)
        LA = moR[:, 0:4 * 527].rearrange("p (g t) -> p g t", g=4)
        LB = moR[:, 2108:2108 + 3 * 527].rearrange("p (g t) -> p g t", g=3)
        KIS = moR[:, 0:1024].rearrange("p (a t) -> p a t", a=2)
        SW = moR[:, 1024:2048]
        ARS = moR[:, 0:1024].rearrange("p (a t) -> p a t", a=2)
        ARP = moR[:, 1024:3072].rearrange("p (a t) -> p a t", a=4)
        ART = moR[:, 3072:4096].rearrange("p (a t) -> p a t", a=2)
        att = sb("att", [P, 4, 4])
        PT = sb("PT", [P, NB, NPG], I32)
        idxI = sb("idxI", [P, NB, NPP], I32)
        phys = sb("phys", [P, 2, NB, NPP])
        base = sb("base", [P, 1])
        qib = sb("qib", [P, NB, 16])
        qb = sb("qb", [P, NB, 8])
        wdiag = sb("wdiag", [8, NB, 8])
        wbc = sb("wbc", [P, NB, 8])
        sdot = sb("sdot", [8, 64])
        snew = sb("snew", [8, 1])
        sTok = sb("sTok", [P, P])
        cols = sb("cols", [64, 16])
        sgn, kth, cntA, cntB, offs, need, snegc = (cols[:, i:i + 1] for i in range(7))
        candI = sb("candI", [64, 2], I32)
        IDX = sb("IDX", [P, NB, 2], I32)
        sm = sb("sm", [64, 8])
        pnd = sb("pnd", [64, 8])
        tmp8 = sb("tmp8", [64, 8])
        pn = sb("pn", [8, 64])

        ps = ctx.enter_context(nc.psum_tensor("ps", [P, 8, 512], F32))

        def main(g):
            return ps[:, 2 * (g % 2):2 * (g % 2) + 2, 0:HT]

        def halves(ap):
            return ap.rearrange("p (f t) -> p f t", f=2)

        const_in = Signal("const_in", 0)
        x_in = Signal("x_in", 0)
        x_turned = Signal("x_turned", 0)
        w_in_slot = [Signal("w_in_slot0", 16 * SLOT_DMAS[0]), Signal("w_in_slot1", 16 * SLOT_DMAS[1])]
        w_val_slot = [Signal(f"w_val_slot{u}", 16 * NF // 2) for u in range(2)]
        vec_in = Signal("vec_in", 16 * 9)
        pages_in = Signal("pages_in", 16 * 64)
        prep_mm = Signal("prep_mm", 1)
        prep_ev = Signal("prep_ev", 4)
        x_ready = Signal("x_ready", 16)
        sq_ready = Signal("sq_ready", 16)
        sq_used = Signal("sq_used", 4 * (KD - 1))
        col_mm = Signal("col_mm", 4)
        col_var = Signal("col_var", 8)
        col_root = Signal("col_root", 4)
        col_ready = Signal("col_ready", 4)
        row_mm = Signal("row_mm", 4)
        rstd_ready = Signal("rstd_ready", 2)
        h_ready = Signal("h_ready", KD)
        hhi_ready = Signal("hhi_ready", KD)
        hlo_ready = Signal("hlo_ready", KD)
        mhi_ready = Signal("mhi_ready", KD)
        mlo_ready = Signal("mlo_ready", KD)
        ohi_ready = Signal("ohi_ready", KD // 2)
        olo_ready = Signal("olo_ready", KD // 2)
        whi_ready = Signal("whi_ready", SPLITS)
        wlo_ready = Signal("wlo_ready", SPLITS)
        yhi_ready = Signal("yhi_ready", NF)
        ylo_ready = Signal("ylo_ready", NF)
        kv_mm = Signal("kv_mm", 5)
        kv_ev = Signal("kv_ev", 5)
        nat_ready = Signal("nat_ready", 2)
        kid_ready = Signal("kid_ready", 1)
        kt_mm = Signal("kt_mm", 3)
        kt_ev = Signal("kt_ev", 4)
        tile_done = Signal("tile_done", TILES, 1)
        evac = Signal("evac", EVACS, 1)
        val_used = Signal("val_used", NF)
        rot_mm = Signal("rot_mm", 8)
        qc_ready = Signal("qc_ready", 8)
        rot_used = Signal("rot_used", 8)
        rope_done = Signal("rope_done", 8)
        dot_mm = Signal("dot_mm", 24)
        dot_relu = Signal("dot_relu", 24)
        dot_acc = Signal("dot_acc", 24)
        sel_ready = Signal("sel_ready", 3)
        qib_mm = Signal("qib_mm", 2)
        qib_ev = Signal("qib_ev", 7)
        wd_ready = Signal("wd_ready", 1)
        pg_mm = Signal("pg_mm", 16)
        pg_ev = Signal("pg_ev", 16)
        sdot_mm = Signal("sdot_mm", 17)
        sw_used = Signal("sw_used", 9)
        stok_ready = Signal("stok_ready", 2)
        sT_mm = Signal("sT_mm", 2)
        sT_ev = Signal("sT_ev", 1)
        cnt_ready = Signal("cnt_ready", 1 + BITS)
        cnt_mm = Signal("cnt_mm", 1 + BITS)
        pick_ready = Signal("pick_ready", 4)
        pick_mm = Signal("pick_mm", 4)
        pos_mm = Signal("pos_mm", 1)
        hot_ready = Signal("hot_ready", 1)
        list_mm = Signal("list_mm", 1)
        list_ev = Signal("list_ev", 1)
        list_ready = Signal("list_ready", 1)
        list_out = Signal("list_out", 16)
        list_in = Signal("list_in", 16)
        kg_in = Signal("kg_in", 16 * 16)
        vg_in = Signal("vg_in", 16 * 16)
        tables = Signal("tables", 0)
        sums_ready = Signal("sums_ready", 9)
        diff_ready = Signal("diff_ready", 8)
        pout_mm = Signal("pout_mm", 1)
        pout_ev = Signal("pout_ev", 1)
        qk_mm = Signal("qk_mm", UNITS)
        qk_used = Signal("qk_used", UNITS)
        neg_max = Signal("neg_max", UNITS)
        exp_done = Signal("exp_done", UNITS)
        prob_ready = Signal("prob_ready", UNITS)
        pt_mm = Signal("pt_mm", UNITS)
        pt_ev = Signal("pt_ev", UNITS)
        pv_mm = Signal("pv_mm", UNITS)
        o_ev = Signal("o_ev", NT)
        ks_mm = Signal("ks_mm", 4)
        ks_ev = Signal("ks_ev", 4)
        qs_mm = Signal("qs_mm", 3)
        qs_ev = Signal("qs_ev", 2)
        ss_ready = Signal("ss_ready", 1)
        se_ready = Signal("se_ready", 1)
        sp_ready = Signal("sp_ready", 2)
        sp_mm = Signal("sp_mm", 1)
        sp_ev = Signal("sp_ev", 2)
        so_mm = Signal("so_mm", 1)
        so_ev = Signal("so_ev", 2, 1)
        upd = Signal("upd", 16)
        gate_ev = Signal("gate_ev", NF)
        conv_done = Signal("conv_done", NF)
        gelu_done = Signal("gelu_done", NF)
        co_mm = Signal("co_mm", NF)
        co_ev = Signal("co_ev", NF, 1)
        out_conv = Signal("out_conv", 16 * 2)
        out_sync = Signal("out_sync", 16 * 10, 1)
        y_mm = Signal("y_mm", 0)
        y_ev = Signal("y_ev", 0)
        y_out = Signal("y_out", 0)
        dve_step = Steps("dve_step", 231)
        passed = {e.engine: Signal(f"passed{i}", 0) for i, e in
                  enumerate((nc.sync, nc.gpsimd, nc.tensor, nc.scalar, nc.vector))}
        ffn_step = Steps("ffn_step", 5)
        pool_step = Signal("pool_step", 1)

        SQUARES_ROOM = (4, 4, KD, 2)

        def squares_at(n, k):
            k %= SQUARES_ROOM[n]
            return SQ[:, k, :] if k < 4 else SEL[:, (k - 4) * TOK:(k - 3) * TOK]

        def gain(a, k):
            return V[:, 8 * a + k:8 * a + k + 1]
        G_PRE_MIX, G_POST_MIX, G_PRE_FFN, G_POST_FFN = range(4)

        def wslot(c):
            return W[:, c % 2, :]

        def pair_w(c):
            return wslot(c)[:, 0:2048].rearrange("p (k n) -> p k n", k=KD)

        x_rows = yR[:, 0:NT * D_MODEL].rearrange("p (t d) -> p t d", t=NT)
        xs_rows = yR[0:NB, 4096:4096 + D_MODEL]

        def wait_alone(eng, sem, value):
            eng.wait_ge(sem, value)
            eng.sem_inc(passed[eng.engine].sem, 1)

        block = ctx.enter_context(nc.Block())
        nc.disable_value_cache = True

        @block.sync
        def _(sp):
            sp.sem_inc(out_sync.sem, 1)
            sp.dma_start(C[:, :], A["consts"]).then_inc(const_in.sem, 16)
            sp.dma_start(PT[:, :, :].rearrange("p b j -> p (b j)"),
                         A["page_table"].rearrange("b j -> (b j)").partition_broadcast(P)).then_inc(const_in.sem, 16)
            sp.dma_start(x_rows, A["x_prompt"][0].rearrange("(t p) d -> p t d", p=P)).then_inc(x_in.sem, 16)
            sp.dma_start(xs_rows, A["x_sample"][:, 0, :]).then_inc(x_in.sem, 16)

            def layer(l):
                w_in = A["w_in"][l].rearrange("(k p) n -> p k n", p=P)

                def load(c):
                    s = w_in_slot[c % 2].sem
                    if c == 0:
                        d = wslot(0)[:, 0:KD * KVW].rearrange("p (k n) -> p k n", k=KD)
                        sp.dma_start(d[:, :, 0:128], w_in[:, :, K0:K0 + 128]).then_inc(s, 16)
                        sp.dma_start(d[:, :, 128:200], w_in[:, :, KI0:KI0 + 72]).then_inc(s, 16)
                        sp.dma_start(d[:, :, 200:328], w_in[:, :, V0:V0 + 128]).then_inc(s, 16)
                    elif c < 5:
                        c0 = (QI0 if c < 3 else XP0) + 256 * ((c - 1) % 2)
                        sp.dma_start(pair_w(c), w_in[:, :, c0:c0 + 256]).then_inc(s, 16)
                    elif c < 7:
                        for u in range(2):
                            for n in range(2):
                                c0 = Q0 + 256 * n + HD * (2 * (c - 5) + u)
                                d = P * u + HD * n
                                sp.dma_start(pair_w(c)[:, :, d:d + HD], w_in[:, :, c0:c0 + HD]).then_inc(s, 16)
                    elif c == 7:
                        sp.dma_start(wslot(7)[:, 0:512].rearrange("p (g d) -> p g d", g=4),
                                     A["w_pool"][l].rearrange("g c d -> c g d")).then_inc(s, 16)
                    else:
                        c0 = 256 * (c - C_WO)
                        w = A["w_out"][l][:, c0:c0 + 256]
                        d = pair_w(c)
                        for n in range(2):
                            sp.dma_start(d[64 * n:64 * n + 64, 0:4, :],
                                         w[256 * n:256 * n + 256, :].rearrange("(j d) n -> d j n", j=4)
                                         ).then_inc(s, 16)
                        sp.dma_start(d[:, 4:8, :], w[512:1024, :].rearrange("(k p) n -> p k n", p=P)
                                     ).then_inc(s, 16)

                wait_alone(sp, *so_ev(l, 0))
                v = vec_rows
                for a, name in enumerate(("g_pre_mix", "g_post_mix", "g_pre_ffn", "g_post_ffn")):
                    sp.dma_start(v[8 * a:8 * a + 8, :], A[name][l].rearrange("(k p) -> k p", p=P)
                                 ).then_inc(vec_in.sem, 16)
                sp.dma_start(v[32:36, :], A["pool_scale"][l].rearrange("(k p) -> k p", p=P)
                             ).then_inc(vec_in.sem, 16)
                sp.dma_start(v[36:102, :], A["conv_w"][l].rearrange("j (k p) -> (j k) p", p=P)
                             ).then_inc(vec_in.sem, 16)
                sp.dma_start(v[102:124, :], A["conv_b"][l].rearrange("(k p) -> k p", p=P)).then_inc(vec_in.sem, 16)
                sp.dma_start(state_rows[0:NB * POOL_BUF, :], A["state_pool"][l].rearrange("b r c -> (b r) c")
                             ).then_inc(vec_in.sem, 16)
                sp.dma_start(conv_rows, A["state_conv"][l].rearrange("b j f -> (b j) f")).then_inc(vec_in.sem, 16)
                wait_alone(sp, *tile_done(l, 0))
                load(0)
                load(1)
                wait_alone(sp, *kv_mm(l, 5))
                load(2)
                for c in (3, 4):
                    wait_alone(sp, *tile_done(l, 2 * (c - 2)))
                    load(c)
                wait_alone(sp, *nat_ready(l, 1))
                for t, name in ((0, "prompt"), (4, "sample")):
                    if t == 0:
                        kvd = [O[f"new_{x}_prompt"][l, 0].rearrange("(t p) n d -> p t (n d)", p=P) for x in "kv"]
                        kid_d = O["new_ik_prompt"][l, 0].rearrange("(t p) d -> p t d", p=P)
                        src = NAT[:, 0:4, :]
                    else:
                        kvd = [O[f"new_{x}_sample"][l, :, 0].rearrange("b n d -> b (n d)") for x in "kv"]
                        kid_d = O["new_ik_sample"][l, :, 0]
                        src = NAT[0:NB, 4, :]
                    at = (lambda a, b: src[:, :, a:b]) if t == 0 else (lambda a, b: src[:, a:b])
                    sp.dma_start(kvd[0], at(0, 128)).then_inc(out_sync.sem, 16)
                    sp.dma_start(kvd[1], at(200, 328)).then_inc(out_sync.sem, 16)
                    sp.dma_start(kid_d, at(128, 192)).then_inc(out_sync.sem, 16)
                for c in (5, 6, 7):
                    wait_alone(sp, *tile_done(l, 2 * (c - 2)))
                    load(c)
                wait_alone(sp, *tile_done(l, PM_T))
                load(8)
                sp.dma_start(O["new_pool_sample"][l, :, 0:14, :], A["state_pool"][l, :, 1:15, :]
                             ).then_inc(out_sync.sem, 16)
                sp.dma_start(O["new_conv_sample"][l, :, 0, :], A["state_conv"][l, :, 1, :]
                             ).then_inc(out_sync.sem, 16)
                wait_alone(sp, *pout_ev(l, 1))
                sp.dma_start(O["new_pool_prompt"][l, 0], POUT[0:15, :]).then_inc(out_sync.sem, 16)
                sp.dma_start(O["new_pool_sample"][l, :, 14, :], POUT2[:, :]).then_inc(out_sync.sem, 16)
                wait_alone(sp, *tile_done(l, WO_T))
                load(9)
                for c in (10, 11):
                    wait_alone(sp, *tile_done(l, WO_T + 2 * (c - 9)))
                    load(c)

                def gate_or_value(i, slot, a):
                    d = W[:, slot, 1024 * a:1024 * (a + 1)].rearrange("p (k n) -> p k n", k=KD)
                    w = A[("w_gate", "w_val")[a]][l].rearrange("(k p) (i n) -> p k i n", p=P, n=P)
                    sp.dma_start(d, w[:, :, i, :]).then_inc((w_in_slot, w_val_slot)[a][slot].sem, 16)

                def down(m, slot):
                    sp.dma_start(wslot(slot)[:, :].rearrange("p (k n) -> p k n", k=NF),
                                 A["w_down"][l].rearrange("(k p) (m n) -> p k m n", p=P, n=P)[:, :, m, :]
                                 ).then_inc(w_in_slot[slot].sem, 16)
                for i in range(2):
                    wait_alone(sp, *tile_done(l, WO_T + 6 + 2 * i))
                    for a in range(2):
                        gate_or_value(i, i, a)
                with sp.Fori(1, NF // 2) as r:
                    for u in range(2):
                        for a in range(2):
                            wait_alone(sp, *tile_done(l, r * 4 + (GV_T - 4 + 2 * u + a + 1)))
                            gate_or_value(r * 2 + u, u, a)
                for m in range(2):
                    wait_alone(sp, *tile_done(l, DN_T - 2 + 2 * m))
                    down(m, m)
                with sp.Fori(1, KD // 2) as m:
                    for u in range(2):
                        wait_alone(sp, *tile_done(l, m * 2 + (DN_T - 1 + u)))
                        down(m * 2 + u, u)
                wait_alone(sp, *co_ev(l, NF))
                sp.dma_start(O["new_conv_prompt"][l, 0], CVO[0:2, :]).then_inc(out_conv.sem, 16)
                sp.dma_start(O["new_conv_sample"][l, :, 1, :], CVO[2:10, :]).then_inc(out_conv.sem, 16)

            with sp.Fori(0, DEPTH) as l:
                layer(l)
            for t in range(NT):
                wait_alone(sp, *y_ev(0, 2 * t + 2))
                sp.dma_start(O["y_prompt"][0, t * P:(t + 1) * P, :], x_rows[:, t, :]).then_inc(y_out.sem, 16)
            wait_alone(sp, *y_ev(0, 10))
            sp.dma_start(O["y_sample"][:, 0, :], xs_rows).then_inc(y_out.sem, 16)
            sp.wait_ge(y_out.sem, 16 * 5)
            sp.wait_ge(out_sync.sem, 16 * 10 * DEPTH + 1)
            sp.wait_ge(out_conv.sem, 16 * 2 * DEPTH)

        @block.gpsimd
        def _(gp):
            page_pairs = A["cache_idx_k"].rearrange("l n (r e) d -> (l n r) (e d)", e=2)
            k_rows = A["cache_k"].rearrange("l n r h d -> (l n r) (h d)")
            v_rows = A["cache_v"].rearrange("l n r h d -> (l n r) (h d)")
            gp.wait_ge(tables.sem, 3)
            gp.wait_ge(x_turned.sem, KD)

            def cos_part(l, j):
                wait_alone(gp, *evac(l, Q_T - 4 + j + 1))
                wait_alone(gp, *rope_done(l, max(j - 1, 4)))
                nc.gpsimd.tensor_tensor(QC[:, j % 2, :], QZ[:, j % 2, :], cosR, ALU.mult
                                        ).then_inc(qc_ready.sem, 1)

            def add_updates(l, at):
                for k in range(KD):
                    wait_alone(gp, *upd(l, at + k + 1))
                    nc.gpsimd.tensor_tensor(xT[:, k, :], xT[:, k, :], mo[:, k, :], ALU.add
                                            ).then_inc(x_ready.sem, 1)

            def layer(l):
                wait_alone(gp, *tile_done(l, 0))
                for j in range(64):
                    nc.gpsimd.indirect_dma_start(
                        IK[:, j, :], None, page_pairs,
                        bass.IndirectOffsetOnAxis(ap=idxI[:, j // NPP, j % NPP:j % NPP + 1], axis=0)
                    ).then_inc(pages_in.sem, 16)
                wait_alone(gp, *rstd_ready(l, 1))
                for j in range(4):
                    wait_alone(gp, *evac(l, XP_T + j + 1))
                    nc.gpsimd.tensor_tensor(XPb[:, j, POOL_BUF:], XPb[:, j, POOL_BUF:], rstd[:, 0:SEQ], ALU.mult
                                            ).then_inc(sums_ready.sem, 1)
                nc.gpsimd.tensor_tensor(XS[:, :, :], XS[:, :, :],
                                        rstd[:, SEQ:TOK].unsqueeze(1).broadcast_to([P, 4, NB]), ALU.mult
                                        ).then_inc(sums_ready.sem, 1)
                wait_alone(gp, *sums_ready(l, 5))
                wait_alone(gp, *stok_ready(l, 2))
                wait_alone(gp, *sdot_mm(l, 17))
                nc.gpsimd.tensor_tensor(LA[:, :, 1:527], XPb[:, :, 1:527], XPb[:, :, 0:526], ALU.add
                                        ).then_inc(sums_ready.sem, 1)
                wait_alone(gp, *sums_ready(l, 6))
                nc.gpsimd.tensor_tensor(LB[:, :, 3:527], LA[:, 1:4, 3:527], LA[:, 1:4, 1:525], ALU.add
                                        ).then_inc(sums_ready.sem, 1)
                wait_alone(gp, *sums_ready(l, 7))
                nc.gpsimd.tensor_tensor(LA[:, 2:4, 7:527], LB[:, 1:3, 7:527], LB[:, 1:3, 3:523], ALU.add
                                        ).then_inc(sums_ready.sem, 1)
                wait_alone(gp, *sums_ready(l, 8))
                nc.gpsimd.tensor_tensor(LB[:, 2, 15:527], LA[:, 3, 15:527], LA[:, 3, 7:519], ALU.add
                                        ).then_inc(sums_ready.sem, 1)
                for j in range(4, 8):
                    cos_part(l, j)
                wait_alone(gp, *pages_in(l, 16 * 64))
                nc.gpsimd.tensor_scalar(idxI[:, :, :], idxI[:, :, :], float(N_PHYS * 64), None, ALU.add
                                        ).then_inc(pool_step.sem, 1)
                wait_alone(gp, *list_ready(l, 1))
                gp.dma_start(scratch.rearrange("b (h i) -> h b i", h=16), ixi[:, :, :]).then_inc(list_out.sem, 16)
                wait_alone(gp, *list_out(l, 16))
                gp.dma_start(IDX[:, :, :], scratch.rearrange("b (p t) -> p b t", t=2)).then_inc(list_in.sem, 16)
                wait_alone(gp, *list_in(l, 16))
                for dst, rows, s in ((KG, k_rows, kg_in), (VG, v_rows, vg_in)):
                    for b in range(NB):
                        for t in range(2):
                            nc.gpsimd.indirect_dma_start(
                                dst[:, 2 * b + t, :], None, rows,
                                bass.IndirectOffsetOnAxis(ap=IDX[:, b, t:t + 1], axis=0)).then_inc(s.sem, 16)
                add_updates(l, 0)
                wait_alone(gp, *pool_step(l, 1))
                add_updates(l, KD)

            with gp.Fori(0, DEPTH) as l:
                layer(l)

        @block.tensor
        def _(pe):
            pe.sem_inc(tile_done.sem, 1)
            mm, turn = nc.tensor.matmul, nc.tensor.transpose

            pe.wait_ge(const_in.sem, 32)
            pe.wait_ge(x_in.sem, 32)
            for k in range(KD):
                if k >= 2:
                    pe.wait_ge(x_ready.sem, k - 1)
                b = 2 * (k % 2)
                for t in range(NT):
                    turn(ps[:, b, t * P:(t + 1) * P], x_rows[:, t, k * P:(k + 1) * P], ident)
                turn(ps[:, b + 1, 0:NB], xs_rows[:, k * P:(k + 1) * P], ident[0:NB, 0:NB]
                     ).then_inc(x_turned.sem, 1)

            def token_sums(l, n):
                pe.wait_ge(*sq_used(l, (KD - 1) * (n + 1)))
                for t in range(5):
                    m = P if t < NT else NB
                    last = mm(ps[0:m, 4, 300 + t:301 + t], SUM[:, t * P:t * P + m], ones[:, 0:1], start=True, stop=True)
                last.then_inc(col_mm.sem, 1)

            def along_tokens(l, n):
                pe.wait_ge(*col_ready(l, n + 1))
                for t in range(5):
                    a, b = t * P, min(t * P + P, TOK)
                    for f in range(2):
                        lo, hi = max(a, f * HT), min(b, (f + 1) * HT)
                        if lo < hi:
                            last = mm(ps[:, 4 + f, lo - f * HT:hi - f * HT], rcol[0:b - a, t:t + 1].broadcast_to([b - a, P]),
                                      ident[0:b - a, lo - a:hi - a], start=True, stop=True)
                last.then_inc(row_mm.sem, 1)

            def arrived(l, c):
                pe.wait_ge(*w_in_slot[c % 2](l, 16 * dmas_before(c)))

            def product(g, lhsT, rhs, nk, extras=None, before=None):
                for k in range(nk):
                    if before:
                        before(k)
                    for f in range(2):
                        last = mm(ps[:, 2 * (g % 2) + f, 0:HT], lhsT(k), rhs[:, k, f * HT:(f + 1) * HT],
                                  start=(k == 0), stop=(k == nk - 1))
                    if extras and k < nk - 1:
                        extras.pop(0)()
                last.then_inc(tile_done.sem, 1)
                if extras:
                    extras.pop(0)()

            def product_in_parts(g, hi, lo, xhi, xlo, nk, before=None):
                for k in range(nk):
                    if before:
                        before(k)
                    for n, (w, x) in enumerate(((hi, xhi), (hi, xlo), (lo, xhi))):
                        for f in range(2):
                            last = mm(ps[:, 2 * (g % 2) + f, 0:HT], w(k), x(k)[:, f * HT:(f + 1) * HT],
                                      start=(k == 0 and n == 0), stop=(k == nk - 1 and n == 2))
                last.then_inc(tile_done.sem, 1)

            def layer(l):
                pe.wait_ge(*vec_in(l, 16 * 9))
                pe.wait_ge(*co_ev(l, 0))
                turn(ps[:, 7, 0:124], vec_rows[0:124, :], ident[0:124, 0:124])
                rows = NB * POOL_BUF
                for g in range(4):
                    mm(ps[:, 7, P + 8 * g:P + 8 * g + 8], state_rows[0:rows, g * P:(g + 1) * P],
                       const("wsel", rows)[:, 8 * g:8 * g + 8], start=True, stop=True)
                for i in range(NF):
                    last = turn(ps[:, 6, 16 * i:16 * i + 16], conv_rows[:, i * P:(i + 1) * P], ident[0:16, 0:16])
                last.then_inc(prep_mm.sem, 1)
                arrived(l, 0)
                wkv = wslot(0)[:, 0:KD * KVW].rearrange("p (k n) -> p k n", k=KD)
                for t in range(5):
                    m, bank = (P, t) if t < NT else (NB, 6)
                    pe.wait_ge(*(evac(l, 0) if t < NT else prep_ev(l, 4)))
                    for k in range(KD):
                        if t == 0:
                            pe.wait_ge(*h_ready(l, k + 1))
                        last = mm(ps[0:m, bank, 0:KVW], hT[:, k, t * P:t * P + m], wkv[:, k, :],
                                  start=(k == 0), stop=(k == KD - 1))
                    last.then_inc(kv_mm.sem, 1)
                    if t == 0:
                        token_sums(l, 0)
                    elif t == 1:
                        along_tokens(l, 0)

                def tile8(g, c, u, rhs=hT, **kw):
                    product(g, lambda k: pair_w(c)[:, k, u * P:(u + 1) * P], rhs, KD, **kw)

                def partner(j):
                    pe.wait_ge(*evac(l, (QI_T if j < 4 else Q_T - 4) + j + 1))
                    if j == 0:
                        pe.wait_ge(*kv_ev(l, 5))
                        pe.wait_ge(*kt_ev(l, 4))
                    elif j == 4:
                        pe.wait_ge(*sw_used(l, 8))
                    else:
                        pe.wait_ge(*rot_used(l, j))
                    for f in range(2):
                        last = mm(ps[:, 6 + f, 0:HT], const("rot"), QZ[:, j % 2, f * HT:(f + 1) * HT],
                                  start=True, stop=True)
                    last.then_inc(rot_mm.sem, 1)

                for j in range(4):
                    if j % 2 == 0:
                        arrived(l, 1 + j // 2)
                    pe.wait_ge(*(kv_ev(l, 2 + 2 * j) if j < 2 else evac(l, j - 1)))
                    tile8(QI_T + j, 1 + j // 2, j % 2)
                    if j == 1:
                        pe.wait_ge(*kid_ready(l, 1))
                        pe.wait_ge(*prep_ev(l, 4))
                        for t in range(NT):
                            last = turn(ps[:, 4, t * P:(t + 1) * P],
                                        kid[:, t, :, :].rearrange("p a d -> p (a d)"), ident)
                        last.then_inc(kt_mm.sem, 1)
                        for t in range(NT):
                            last = turn(ps[:, 5, t * P:(t + 1) * P], NAT[:, t, 0:P], ident)
                        last.then_inc(kt_mm.sem, 1)
                        turn(ps[:, 7, 0:NB], kid[0:NB, 4, :, :].rearrange("p a d -> p (a d)"), ident[0:NB, 0:NB])
                        turn(ps[:, 7, 8:8 + NB], NAT[0:NB, 4, 0:P], ident[0:NB, 0:NB]).then_inc(kt_mm.sem, 1)
                        partner(0)
                    elif j >= 2:
                        partner(j - 1)
                partner(3)

                arrived(l, 3)
                pe.wait_ge(*evac(l, XP_T - 1))
                tile8(XP_T, 3, 0)

                for d in range(24):
                    t, h = 1 + d // 8, d % 8
                    if d == 0:
                        pe.wait_ge(*rope_done(l, 4))
                        pe.wait_ge(*kt_ev(l, 4))
                    if d >= 2:
                        pe.wait_ge(*dot_relu(l, d - 1))
                    rows = slice(64 * (h % 2), 64 * (h % 2) + 64)
                    mm(ps[:, 4 + d % 2, 0:P * (t + 1)], qiT[rows, h // 2, t * P:(t + 1) * P],
                       kiT[rows, 0:P * (t + 1)], start=True, stop=True).then_inc(dot_mm.sem, 1)
                    k = d % KD
                    if k == 0:
                        if t == 2:
                            arrived(l, 4)
                        pe.wait_ge(*evac(l, XP_T + t - 1))
                    for f in range(2):
                        last = mm(ps[:, 2 * (t % 2) + f, 0:HT], pair_w(3 + t // 2)[:, k, t % 2 * P:(t % 2 + 1) * P],
                                  hT[:, k, f * HT:(f + 1) * HT], start=(k == 0), stop=(k == KD - 1))
                    if k == KD - 1:
                        last.then_inc(tile_done.sem, 1)

                pe.wait_ge(*rot_used(l, 4))
                mm(ps[:, 6, 0:32], const("swap"), qiT[:, 0:4, SEQ:TOK], start=True, stop=True
                   ).then_inc(qib_mm.sem, 1)
                pe.wait_ge(*wd_ready(l, 1))
                mm(ps[:, 7, 0:64], ones[0:8, :], wdiag[:, :, :].rearrange("p b h -> p (b h)"),
                   start=True, stop=True).then_inc(qib_mm.sem, 1)

                def page_products(g):
                    pe.wait_ge(*pg_ev(l, g + 1))
                    for i in range(4):
                        q = 4 * g + i
                        last = mm(ps[:, 6 + q // 32, 16 * (q % 32):16 * (q % 32) + 16],
                                  KIS[:, g % 2, i * P:(i + 1) * P], qib[:, q // NPP, :], start=True, stop=True)
                    last.then_inc(sdot_mm.sem, 1)

                pe.wait_ge(*pages_in(l, 16 * 64))
                for g in range(16):
                    pe.wait_ge(*(dot_relu(l, 24) if g < 2 else pg_ev(l, g - 1)))
                    for i in range(4):
                        last = turn(ps[:, 4 + g % 2, i * P:(i + 1) * P], IK[:, 4 * g + i, :], ident)
                    last.then_inc(pg_mm.sem, 1)
                    if g == 1:
                        pe.wait_ge(*qib_ev(l, 5))
                    if g >= 1:
                        page_products(g - 1)
                page_products(15)
                mm(ps[0:NB, 4, 0:64], kiT[0:64, SEQ:TOK], qib[0:64, :, 0:8], start=True, stop=True
                   ).then_inc(sdot_mm.sem, 1)

                def scores_turned():
                    wait_alone(pe, *stok_ready(l, 2))
                    for e in range(2):
                        last = turn(ps[0:64, 4, e * P:(e + 1) * P], sTok[:, e:P:2], ident)
                    last.then_inc(sT_mm.sem, 1)
                    mm(ps[0:64, 5, 0:1], const("newrow", 8), snew[:, :], start=True, stop=True
                       ).then_inc(sT_mm.sem, 1)

                def count(s):
                    def go():
                        wait_alone(pe, *cnt_ready(l, s + 1))
                        mm(ps[0:64, 4 + s % 2, 300:301], const("same", 64), (cntB if s % 2 else cntA),
                           start=True, stop=True).then_inc(cnt_mm.sem, 1)
                    return go

                extras = [scores_turned] + [count(s) for s in range(1 + BITS)]
                for j in range(4):
                    if j % 2 == 0:
                        arrived(l, 5 + j // 2)
                    pe.wait_ge(*evac(l, Q_T + j - 1))
                    tile8(Q_T + j, 5 + j // 2, j % 2, extras=extras)
                    if j >= 1:
                        partner(3 + j)
                partner(7)
                for step in extras:
                    step()
                pe.wait_ge(*rot_used(l, 8))
                for g in range(4):
                    turn(ps[0:15, 6, g * P:(g + 1) * P], XPb[:, g, 512:527], ident)
                for g in range(4):
                    last = turn(ps[0:NB, 7, g * P:(g + 1) * P], XS[:, g, :], ident)
                last.then_inc(pout_mm.sem, 1)
                arrived(l, 7)
                wp = wslot(7)[:, 0:512].rearrange("p (g d) -> p g d", g=4)
                for g in range(4):
                    pe.wait_ge(*evac(l, PM_T + g - 1))
                    pe.wait_ge(*diff_ready(l, 2 * g + 2))
                    for f in range(2):
                        last = mm(ps[:, 2 * (g % 2) + f, 0:HT], wp[:, g, :], DIFF[:, g, f * HT:(f + 1) * HT],
                                  start=True, stop=True)
                    last.then_inc(tile_done.sem, 1)

                def pick_a():
                    wait_alone(pe, *pick_ready(l, 2))
                    wait_alone(pe, *evac(l, WO_T))
                    mm(ps[0:64, 3, 0:1], const("same", 64), cntA, start=True, stop=True).then_inc(pick_mm.sem, 1)
                    mm(ps[0:64, 3, 1:2], const("below", 64), cntB, start=True, stop=True).then_inc(pick_mm.sem, 1)

                def pick_b():
                    wait_alone(pe, *pick_ready(l, 3))
                    mm(ps[0:64, 3, 2:3], const("below", 64), cntA, start=True, stop=True).then_inc(pick_mm.sem, 1)
                    mm(ps[0:64, 3, 3:4], const("newto", 64), J[:, 256:257], start=True, stop=True
                       ).then_inc(pick_mm.sem, 1)

                def pick_c():
                    wait_alone(pe, *pick_ready(l, 4))
                    for g in range(2):
                        last = turn(ps[:, 3, P + 64 * g:P + 64 * g + 64], S2[:, g * P:(g + 1) * P],
                                    ident[0:64, 0:64])
                    last.then_inc(pos_mm.sem, 1)

                def pick_d():
                    wait_alone(pe, *hot_ready(l, 1))
                    for b in range(NB):
                        for g in range(2):
                            for pp in range(NPP):
                                c = 64 * g + NPP * b + pp
                                last = mm(ps[0:16, 3, 256 + 32 * b:288 + 32 * b], OA[:, c, :],
                                          OB[:, c, :, :].rearrange("p w i -> p (w i)"),
                                          start=(g == 0 and pp == 0), stop=(g == 1 and pp == NPP - 1))
                    last.then_inc(list_mm.sem, 1)

                def keys_turned(q):
                    if q == 0:
                        wait_alone(pe, *kg_in(l, 16 * 16))
                    wait_alone(pe, *(list_ev(l, 1) if q == 0 else ks_ev(l, q)))
                    for i in range(4):
                        last = turn(ps[:, 3, i * P:(i + 1) * P], KG[:, 4 * q + i, :], ident)
                    last.then_inc(ks_mm.sem, 1)

                def sample_scores():
                    wait_alone(pe, *ks_ev(l, 4))
                    wait_alone(pe, *qib_ev(l, 7))
                    for b in range(NB):
                        for t in range(2):
                            last = mm(ps[:, 3, 64 * t + 8 * b:64 * t + 8 * b + 8], KTS[:, 2 * b + t, :], qb[:, b, :],
                                      start=True, stop=True)
                    last.then_inc(qs_mm.sem, 1)

                def scores_by_row():
                    wait_alone(pe, *qs_ev(l, 1))
                    for t in range(2):
                        last = turn(ps[0:64, 3, P * (t + 1):P * (t + 2)], sc2[:, 64 * t:64 * t + 64], ident)
                    last.then_inc(qs_mm.sem, 1)
                    mm(ps[0:64, 3, 400:408], qb[:, :, :].rearrange("p b h -> p (b h)"), kT[:, SEQ:TOK],
                       start=True, stop=True).then_inc(qs_mm.sem, 1)

                picks = {1: pick_a, 3: pick_b, 5: pick_c, 9: pick_d, 30: sample_scores, 32: scores_by_row}
                picks.update({25 + q: (lambda q=q: keys_turned(q)) for q in range(4)})

                def scores(i):
                    t, h = divmod(i, N_HEADS)
                    rows = slice(64 * (h // 4), 64 * (h // 4) + 64)
                    if i == 0:
                        pe.wait_ge(*rope_done(l, 8))
                        pe.wait_ge(*evac(l, WO_T))
                    if i >= 3:
                        pe.wait_ge(*qk_used(l, i - 2))
                    mm(ps[:, i % 3, 0:P * (t + 1)], qT[rows, h % 4, t * P:(t + 1) * P],
                       kT[rows, 0:P * (t + 1)], start=True, stop=True).then_inc(qk_mm.sem, 1)

                def turn_probs(i):
                    t = i // N_HEADS
                    pe.wait_ge(*prob_ready(l, i + 1))
                    if i >= 2:
                        pe.wait_ge(*pt_ev(l, i - 1))
                    for kt in range(t + 1):
                        last = turn(ps[:, 4 + i % 2, kt * P:(kt + 1) * P], ARP[:, i % 4, kt * P:(kt + 1) * P], ident)
                    last.then_inc(pt_mm.sem, 1)

                def values(i):
                    t, h = divmod(i, N_HEADS)
                    n, j = divmod(h, 4)
                    pe.wait_ge(*pt_ev(l, i + 1))
                    if i == 0:
                        pe.wait_ge(*pout_ev(l, 1))
                    if h == 0 and t >= 2:
                        pe.wait_ge(*o_ev(l, t - 1))
                    for kt in range(t + 1):
                        last = mm(ps[64 * n:64 * n + 64, 6 + t % 2, j * P:(j + 1) * P],
                                  NAT[:, kt, 200 + 64 * n:264 + 64 * n], ART[:, i % 2, kt * P:(kt + 1) * P],
                                  start=(kt == 0), stop=(kt == t))
                    last.then_inc(pv_mm.sem, 1)

                for i in range(UNITS + 3):
                    if i < UNITS:
                        scores(i)
                    if i in picks:
                        picks[i]()
                    if 2 <= i < UNITS + 2:
                        turn_probs(i - 2)
                    if i >= 3:
                        values(i - 3)

                wait_alone(pe, *sp_ready(l, 2))
                for t in range(2):
                    turn(ps[:, 3, 64 * t:64 * t + 64], PA[:, P * t:P * (t + 1)], ident[0:64, 0:64])
                turn(ps[0:8, 3, P:P + 64], pnd[:, :], ident[0:64, 0:64]).then_inc(sp_mm.sem, 1)
                wait_alone(pe, *sp_ev(l, 2))
                wait_alone(pe, *vg_in(l, 16 * 16))
                mm(ps[:, 3, 256:320], NAT[0:NB, 4, 200:328], pn[:, :], start=True, stop=False,
                   skip_group_check=True)
                for b in range(NB):
                    for t in range(2):
                        last = mm(ps[:, 3, 256 + 8 * b:264 + 8 * b], VG[:, 2 * b + t, :],
                                  pT2[:, t, 8 * b:8 * b + 8], start=False,
                                  stop=(b == NB - 1 and t == 1), skip_group_check=True)
                last.then_inc(so_mm.sem, 1)

                pe.wait_ge(*qk_used(l, UNITS))
                for m in range(KD):
                    if m >= 2:
                        pe.wait_ge(*evac(l, WO_T + m - 1))
                    pe.wait_ge(*olo_ready(l, m // 2 + 1))
                    slot, u = m // 2 % 2, m % 2

                    def part(k):
                        at = 256 * MIX_ORDER[k] + P * u
                        return slice(at, at + P)
                    product_in_parts(WO_T + m, lambda k: OH[slot][:, part(k)],
                                     lambda k: lower_w(slot, part(k).start, part(k).stop),
                                     lambda k: MH[MIX_ORDER[k]], lambda k: tile_of("hT", MIX_ORDER[k]), KD,
                                     (lambda k: pe.wait_ge(*mlo_ready(l, k + 1))) if m == 0 else None)
                token_sums(l, 1)
                along_tokens(l, 1)

                def gate_value(i, u, first):
                    def parts(g, before=None):
                        pe.wait_ge(*wlo_ready(l, i * 2 + (g + 1)))
                        product_in_parts(g, lambda k: WH[u][:, 1024 * g + P * k:1024 * g + P * (k + 1)],
                                         lambda k: lower_w(u, 1024 * g + P * k, 1024 * g + P * (k + 1)),
                                         lambda k: tile_of("moR", k), lambda k: tile_of("hT", k), KD, before)
                    at_start = first and u == 0
                    if at_start:
                        pe.wait_ge(*evac(l, GV_T))
                    else:
                        pe.wait_ge(*gate_ev(l, i))
                    parts(0, (lambda k: pe.wait_ge(*hlo_ready(l, k + 1))) if at_start else None)
                    if not at_start:
                        pe.wait_ge(*val_used(l, i))

                    def norm_between(k):
                        if k == 3:
                            token_sums(l, 2)
                        elif k == 6:
                            along_tokens(l, 2)
                    parts(1, norm_between if at_start else None)
                    pe.wait_ge(*gate_ev(l, i + 1))
                    if not first:
                        pe.wait_ge(*co_ev(l, i - 1))
                    turn(ps[0:10, 6 + u, 0:P], G[:, u, 512:522], ident).then_inc(co_mm.sem, 1)

                for u in range(2):
                    gate_value(u, u, True)
                with pe.Fori(1, NF // 2) as r:
                    for u in range(2):
                        gate_value(r * 2 + u, u, False)

                for m in range(KD):
                    if m < 2:
                        pe.wait_ge(*val_used(l, NF))
                        pe.wait_ge(*gate_ev(l, NF))
                    else:
                        pe.wait_ge(*evac(l, EVAC_DN + m - 1))

                    def there(k):
                        if k in (0, 16):
                            pe.wait_ge(*wlo_ready(l, 2 * NF + 2 * m + (2 if k else 1)))
                        if m == 0:
                            pe.wait_ge(*ylo_ready(l, k + 1))

                    def upper(k):
                        for k0, at, n in DH[m % 2][0] + DH[m % 2][1]:
                            if k0 <= k < k0 + n:
                                return at[:, P * (k - k0):P * (k - k0 + 1)]
                    product_in_parts(DN_T + m, upper, lambda k: lower_w(m % 2, k * P, (k + 1) * P),
                                     lambda k: YH[k], lambda k: tile_of("yR", k), NF, there)
                token_sums(l, 3)
                along_tokens(l, 3)

            with pe.Fori(0, DEPTH) as l:
                layer(l)
            for n in range(10):
                t, half = divmod(n, 2)
                m = P if t < NT else NB
                if n == 0:
                    pe.wait_ge(*x_ready(DEPTH, KD))
                if n >= 4:
                    pe.wait_ge(y_ev.sem, n - 3)
                for i in range(4):
                    last = turn(ps[0:m, n % 4, i * P:(i + 1) * P], xT[:, 4 * half + i, t * P:t * P + m], ident)
                last.then_inc(y_mm.sem, 1)

        @block.scalar
        def _(act):
            for signal in (evac, so_ev, co_ev):
                act.sem_inc(signal.sem, 1)

            def copy(out, in_):
                return nc.scalar.activation(out, in_, ACT.Copy)

            for k in range(KD):
                act.wait_ge(x_turned.sem, k + 1)
                b = 2 * (k % 2)
                copy(xT[:, k, 0:SEQ], ps[:, b, :])
                copy(xT[:, k, SEQ:TOK], ps[:, b + 1, 0:NB]).then_inc(x_ready.sem, 1)

            def roots(l, n):
                act.wait_ge(*col_var(l, 2 * n + 2))
                nc.scalar.activation(rcol[:, :], rcol[:, :], ACT.Sqrt).then_inc(col_root.sem, 1)

            def rstd_copied(l, n):
                act.wait_ge(*row_mm(l, n + 1))
                copy(halves(rstd[:, :]), ps[:, 4:6, 0:HT]).then_inc(rstd_ready.sem, 1)

            def square_free(l, n, k):
                room = SQUARES_ROOM[n]
                if k >= room:
                    act.wait_ge(*sq_used(l, (KD - 1) * n + max(k - room, 1)))

            def h_and_squares(l, n, gain_of, h, signal):
                for k in range(KD):
                    act.wait_ge(*x_ready(l, 4 * n + k + 1))
                    nc.scalar.activation(h(k), xT[:, k, :], ACT.Copy, scale=gain_of(k)).then_inc(signal.sem, 1)
                    square_free(l, n, k)
                    nc.scalar.activation(squares_at(n, k), xT[:, k, :], ACT.Square).then_inc(sq_ready.sem, 1)

            def upper(out, in_, signal):
                copy(out, in_).then_inc(signal.sem, 1)

            def output_tile(l, n, g, k):
                act.wait_ge(*tile_done(l, g + 1))
                square_free(l, n, k)
                copy(halves(mo[:, k, :]), main(g))
                nc.scalar.activation(halves(squares_at(n, k)), main(g), ACT.Square).then_inc(evac.sem, 1)

            def layer(l):
                act.wait_ge(*prep_mm(l, 1))
                copy(gpm[:, :], ps[:, 7, KD * G_PRE_MIX:KD * (G_PRE_MIX + 1)]).then_inc(prep_ev.sem, 1)
                act.wait_ge(*prep_ev(l, 1))
                h_and_squares(l, 0, lambda k: gpm[:, k:k + 1], lambda k: hT[:, k, :], h_ready)
                copy(V[:, 0:124], ps[:, 7, 0:124]).then_inc(prep_ev.sem, 1)
                copy(prevs[:, :], ps[:, 7, P:P + 32]).then_inc(prep_ev.sem, 1)
                copy(conv_T[:, :, :].rearrange("p i c -> p (i c)"), ps[:, 6, 0:16 * NF]).then_inc(prep_ev.sem, 1)
                roots(l, 0)
                act.wait_ge(*col_ready(l, 1))
                act.wait_ge(*out_sync(l, 0))
                for t in range(5):
                    m, bank = (P, t) if t < NT else (NB, 6)
                    act.wait_ge(*kv_mm(l, t + 1))
                    nc.scalar.activation(NAT[0:m, t, :], ps[0:m, bank, 0:KVW], ACT.Copy, scale=rcol[0:m, t:t + 1]
                                         ).then_inc(kv_ev.sem, 1)
                    if t == 1:
                        rstd_copied(l, 0)

                def q_copy(j, g):
                    act.wait_ge(*tile_done(l, g + 1))
                    if j >= 2:
                        act.wait_ge(*rot_mm(l, j - 1))
                        act.wait_ge(*qc_ready(l, j - 1))
                    copy(halves(QZ[:, j % 2, :]), main(g)).then_inc(evac.sem, 1)

                q_copy(0, QI_T)
                q_copy(1, QI_T + 1)
                act.wait_ge(*nat_ready(l, 1))
                for a in range(2):
                    ki2 = copy(kid[:, :, a, :], NAT[:, :, 128:192])
                ki2.then_inc(kid_ready.sem, 1)
                act.wait_ge(*kt_mm(l, 1))
                copy(kiT[:, 0:SEQ], ps[:, 4, :]).then_inc(kt_ev.sem, 1)
                act.wait_ge(*kt_mm(l, 2))
                copy(kT[:, 0:SEQ], ps[:, 5, :]).then_inc(kt_ev.sem, 1)
                act.wait_ge(*kt_mm(l, 3))
                copy(kiT[:, SEQ:TOK], ps[:, 7, 0:NB]).then_inc(kt_ev.sem, 1)
                copy(kT[:, SEQ:TOK], ps[:, 7, 8:8 + NB]).then_inc(kt_ev.sem, 1)
                q_copy(2, QI_T + 2)
                q_copy(3, QI_T + 3)

                def xp_copy(j):
                    act.wait_ge(*tile_done(l, XP_T + j + 1))
                    X = ps[:, 2 * (j % 2):2 * (j % 2) + 2, :]
                    copy(XPb[:, j, POOL_BUF:POOL_BUF + HT], X[:, 0, 0:HT])
                    copy(XPb[:, j, POOL_BUF + HT:], X[:, 1, 0:SEQ - HT])
                    copy(XS[:, j, :], X[:, 1, SEQ - HT:HT]).then_inc(evac.sem, 1)

                xp_copy(0)
                for d in range(24):
                    n = P * (2 + d // 8)
                    act.wait_ge(*dot_mm(l, d + 1))
                    if d >= 4:
                        act.wait_ge(*dot_acc(l, d - 3))
                    nc.scalar.activation(RB[:, d % 4, 0:n], ps[:, 4 + d % 2, 0:n], ACT.Relu).then_inc(dot_relu.sem, 1)
                    if d % KD == KD - 1:
                        xp_copy(1 + d // KD)
                act.wait_ge(*qib_mm(l, 1))
                q = qib[:, :, :]
                heads = "p b (j two) -> p two j b"
                lo, hi = slice(0, 64), slice(64, 128)
                low = q[lo, :, 0:8].rearrange(heads, two=2)
                high = q[hi, :, 8:16].rearrange(heads, two=2)
                swapped = ps[:, 6, 0:32].rearrange("p (j b) -> p j b", j=4)
                copy(low[:, 0], qiT[lo, :, SEQ:TOK]).then_inc(qib_ev.sem, 1)
                copy(low[:, 1], swapped[lo]).then_inc(qib_ev.sem, 1)
                copy(high[:, 1], qiT[hi, :, SEQ:TOK]).then_inc(qib_ev.sem, 1)
                copy(high[:, 0], swapped[hi]).then_inc(qib_ev.sem, 1)
                act.wait_ge(*qib_mm(l, 2))
                copy(wbc[:, :, :].rearrange("p b h -> p (b h)"), ps[:, 7, 0:64]).then_inc(qib_ev.sem, 1)
                for g in range(16):
                    act.wait_ge(*pg_mm(l, g + 1))
                    if g >= 2:
                        act.wait_ge(*sdot_mm(l, g - 1))
                    copy(KIS[:, g % 2, :], ps[:, 4 + g % 2, :]).then_inc(pg_ev.sem, 1)
                act.wait_ge(*sT_mm(l, 1))
                copy(S[:, 0:256].rearrange("p (r e) -> p e r", e=2),
                     ps[0:64, 4, 0:256].rearrange("p (e r) -> p e r", e=2)).then_inc(sT_ev.sem, 1)
                for j in range(4):
                    q_copy(4 + j, Q_T + j)
                act.wait_ge(*pout_mm(l, 1))
                act.wait_ge(*qc_ready(l, 8))
                copy(POUT[0:15, :], ps[0:15, 6, :])
                copy(POUT2[:, :], ps[0:NB, 7, :]).then_inc(pout_ev.sem, 1)
                for g in range(4):
                    act.wait_ge(*tile_done(l, PM_T + g + 1))
                    nc.scalar.activation(halves(hT[:, 4 + g, :]), main(g), ACT.Copy, scale=V[:, 32 + g:33 + g]
                                         ).then_inc(evac.sem, 1)
                act.wait_ge(*rope_done(l, 8))
                copy(qb[lo, :, 0:4].rearrange("p b j -> p j b"), qT[lo, :, SEQ:TOK]).then_inc(qib_ev.sem, 1)
                copy(qb[hi, :, 4:8].rearrange("p b j -> p j b"), qT[hi, :, SEQ:TOK]).then_inc(qib_ev.sem, 1)

                def exponentials(i):
                    n = P * (1 + i // N_HEADS)
                    act.wait_ge(*neg_max(l, i + 1))
                    if i >= 4:
                        act.wait_ge(*pt_mm(l, i - 3))
                    a = att[:, i % 4, :]
                    nc.scalar.activation(ARP[:, i % 4, 0:n], ARS[:, i % 2, 0:n], ACT.Exp, bias=a[:, 0:1],
                                         accum_out=a[:, 1:2]).then_inc(exp_done.sem, 1)

                def probs_copied(i):
                    n = P * (1 + i // N_HEADS)
                    act.wait_ge(*pt_mm(l, i + 1))
                    if i >= 2:
                        act.wait_ge(*pv_mm(l, i - 1))
                    copy(ART[:, i % 2, 0:n], ps[:, 4 + i % 2, 0:n]).then_inc(pt_ev.sem, 1)

                def upper_out(c):
                    act.wait_ge(*w_in_slot[c % 2](l, 16 * dmas_before(C_WO + c)))
                    upper(OH[c % 2], wslot(c)[:, 0:2048], ohi_ready)

                def upper_mixed(k):
                    k = MIX_ORDER[k]
                    upper(MH[k], hT[:, k, :], mhi_ready)

                for i in range(UNITS + 3):
                    if 26 <= i < 30:
                        q = i - 26
                        act.wait_ge(*ks_mm(l, q + 1))
                        copy(KTS[:, 4 * q:4 * q + 4, :].rearrange("p j d -> p (j d)"), ps[:, 3, :]).then_inc(ks_ev.sem, 1)
                    elif i == 31:
                        act.wait_ge(*qs_mm(l, 1))
                        copy(sc2[:, :], ps[:, 3, 0:P]).then_inc(qs_ev.sem, 1)
                    elif i == 33:
                        act.wait_ge(*qs_mm(l, 3))
                        copy(SA[:, 0:256], ps[0:64, 3, P:3 * P]).then_inc(qs_ev.sem, 1)
                    if i < UNITS:
                        exponentials(i)
                    if 2 <= i < UNITS + 2:
                        probs_copied(i - 2)
                    if i >= 3 and (i - 3) % N_HEADS == N_HEADS - 1:
                        t = (i - 3) // N_HEADS
                        act.wait_ge(*pv_mm(l, i - 2))
                        copy(hT[:, 0:4, t * P:(t + 1) * P], ps[:, 6 + t % 2, :].rearrange("p (j q) -> p j q", j=4)
                             ).then_inc(o_ev.sem, 1)
                    if i in (14, 16, 18, 20):
                        if i == 14:
                            act.wait_ge(*evac(l, WO_T))
                        upper_mixed(i // 2 - 7)
                    if i == 12:
                        act.wait_ge(*list_mm(l, 1))
                        copy(ix[:, :, :, :], ps[0:16, 3, 256:512].rearrange("p (b w i) -> p w b i", w=2, i=16)
                             ).then_inc(list_ev.sem, 1)
                act.wait_ge(*ss_ready(l, 1))
                nc.scalar.activation(PA[:, :], SA[:, :], ACT.Exp, bias=sm[:, 0:1], accum_out=sm[:, 1:2]
                                     ).then_inc(se_ready.sem, 1)
                act.wait_ge(*out_sync(l, 16 * 10))
                upper_out(0)
                act.wait_ge(*sp_mm(l, 1))
                copy(pT2[:, :, :].rearrange("p t c -> p (t c)"), ps[:, 3, 0:P]).then_inc(sp_ev.sem, 1)
                copy(pn[:, :], ps[0:8, 3, P:P + 64]).then_inc(sp_ev.sem, 1)
                act.wait_ge(*so_mm(l, 1))
                for n in range(2):
                    r = slice(64 * n, 64 * n + 64)
                    o = ps[r, 3, 256:320].rearrange("p (b h) -> p h b", b=NB)
                    copy(hT[r, 0:4, SEQ:TOK], o[:, 4 * n:4 * n + 4, :]).then_inc(so_ev.sem, 1)

                def upper_weights(i, r, u, a, first=False):
                    if a:
                        act.wait_ge(w_val_slot[u].sem, l * w_val_slot[u].per + r * 16 + 16)
                    else:
                        act.wait_ge(w_in_slot[u].sem, l * w_in_slot[u].per + r * 16 + 16 * (dmas_before(C_GV - 2 + u) + 1))
                    if not first:
                        act.wait_ge(*tile_done(l, i * 2 + (GV_T - 4 + a + 1)))
                    upper(WH[u][:, 1024 * a:1024 * (a + 1)], W[:, u, 1024 * a:1024 * (a + 1)], whi_ready)

                def upper_down(m):
                    act.wait_ge(*w_in_slot[m % 2](l, 16 * dmas_before(C_DN + m)))
                    if m < 2:
                        act.wait_ge(*tile_done(l, DN_T - 2 + 2 * m))
                    for part in DH[m % 2]:
                        for k0, at, n in part:
                            last = copy(at, wslot(m)[:, P * k0:P * (k0 + n)])
                        last.then_inc(whi_ready.sem, 1)

                def upper_y(tiles):
                    for k in tiles:
                        act.wait_ge(*val_used(l, k + 1))
                        upper(YH[k], yT[:, k, :], yhi_ready)

                act.wait_ge(*so_ev(l, 2))
                for k in range(4, KD):
                    upper_mixed(k)
                upper_out(1)
                for m in range(KD):
                    if m in (2, 4):
                        upper_out(m // 2 + 1)
                    if m == KD - 1:
                        for a in range(2):
                            upper_weights(0, 0, 0, a, True)
                    output_tile(l, 1, WO_T + m, m)
                roots(l, 1)
                h_and_squares(l, 2, lambda k: gain(G_PRE_FFN, k), lambda k: tile_of("moR", k), hhi_ready)
                act.wait_ge(*sq_used(l, (KD - 1) * 3))
                for a in range(2):
                    upper_weights(1, 0, 1, a, True)
                roots(l, 2)
                rstd_copied(l, 2)

                def gate_tile(i, u, first):
                    act.wait_ge(*conv_done(l, i + 1))
                    if not first:
                        act.wait_ge(*val_used(l, i - 1))
                    nc.scalar.activation(GE[:, u, :], CV[:, u, :], ACT.Gelu_apprx_tanh).then_inc(gelu_done.sem, 1)
                    act.wait_ge(*co_mm(l, i + 1))
                    out = CVO[:, :].rearrange("p (i n) -> p i n", n=P)
                    copy(out[:, i:i + 1, :] if isinstance(i, int) else out[:, bass.ds(i, 1), :],
                         ps[0:10, 6 + u, 0:P].rearrange("p (a n) -> p a n", a=1)).then_inc(co_ev.sem, 1)

                gate_tile(0, 0, True)
                for a in range(2):
                    upper_weights(2, 1, 0, a)
                gate_tile(1, 1, True)
                with act.Fori(1, NF // 2 - 1) as r:
                    for u in range(2):
                        for a in range(2):
                            upper_weights(r * 2 + (u + 1), r + u, 1 - u, a)
                        gate_tile(r * 2 + u, u, False)
                upper_weights(NF - 1, NF // 2 - 1, 1, 0)
                upper_y(range(0, 3))
                upper_weights(NF - 1, NF // 2 - 1, 1, 1)
                gate_tile(NF - 2, 0, False)
                upper_y(range(3, 6))
                gate_tile(NF - 1, 1, False)
                upper_down(0)
                act.wait_ge(*val_used(l, NF))
                act.wait_ge(*tile_done(l, DN_T))
                upper_y(range(6, NF))
                upper_down(1)
                for m in range(KD):
                    output_tile(l, 3, DN_T + m, m)
                    if m + 2 < KD:
                        upper_down(m + 2)
                roots(l, 3)

            with act.Fori(0, DEPTH) as l:
                layer(l)
            for n in range(10):
                t, half = divmod(n, 2)
                act.wait_ge(y_mm.sem, n + 1)
                dst = x_rows[:, t, :] if t < NT else xs_rows
                m = P if t < NT else NB
                copy(dst[0:m, 512 * half:512 * half + 512], ps[0:m, n % 4, :]).then_inc(y_ev.sem, 1)

        @block.vector
        def _(dve):
            tt, ts, stt = nc.vector.tensor_tensor, nc.vector.tensor_scalar, nc.vector.scalar_tensor_tensor

            nc.vector.memset(qib[:, :, :], 0.0)
            nc.vector.memset(qb[:, :, :], 0.0)
            nc.vector.memset(base[:, :], 0.0)
            nc.vector.memset(rcol[:, :], 1.0)
            dve.wait_ge(const_in.sem, 32)
            for g in range(2):
                r = slice(64 * g, 64 * g + 64)
                ts(idxI[r, :, :], PT[r, :, g:NPG:2], 64.0, const("row64")[r], ALU.mult, ALU.add
                   ).then_inc(tables.sem, 1)
            nc.vector.tensor_copy(phys[:, :, :, :], PT[:, :, :].rearrange("p b (j two) -> p two b j", two=2)
                                  ).then_inc(tables.sem, 1)

            def sum_squares(l, n, ready, before=None):
                for k in range(1, KD):
                    if before:
                        before(k)
                    dve.wait_ge(*ready(k))
                    if k >= 2:
                        dve.wait_ge(*sq_used(l, (KD - 1) * n + k - 1))
                    tt(SUM[:, :], (SUM if k >= 2 else SQ[:, 0])[:, :], squares_at(n, k), ALU.add).then_inc(sq_used.sem, 1)


            def inverse_root(l, n):
                dve.wait_ge(*col_mm(l, n + 1))
                for r, c in ((P, slice(0, NT)), (NB, slice(NT, NT + 1))):
                    ts(rcol[0:r, c], ps[0:r, 4, 300:305][:, c], 1.0 / D_MODEL, EPS, ALU.mult, ALU.add
                       ).then_inc(col_var.sem, 1)
                dve.wait_ge(*col_root(l, n + 1))
                nc.vector.reciprocal(rcol[:, :], rcol[:, :]).then_inc(col_ready.sem, 1)

            def update(l, n, a, ready, before=None, after=None):
                sum_squares(l, n, ready, before)
                inverse_root(l, n)
                dve.wait_ge(*row_mm(l, n + 1))
                for k in range(KD):
                    stt(halves(mo[:, k, :]), halves(mo[:, k, :]), gain(a, k), ps[:, 4:6, 0:HT], ALU.mult, ALU.mult
                        ).then_inc(upd.sem, 1)
                    if after:
                        after(k)

            def layer(l):
                st = dve_step
                st.begin(l)

                def then_wait(ins):
                    st.add(ins)
                    wait_alone(dve, *st.last())

                nc.vector.memset(XPb[:, :, 0:POOL_BUF], 0.0)
                nc.vector.memset(NAT[:, NT, :], 0.0)
                sum_squares(l, 0, lambda k: sq_ready(l, k + 1))
                inverse_root(l, 0)
                dve.wait_ge(*rstd_ready(l, 1))
                st.add(tt(cosR, const("cosT"), rstd[:, :], ALU.mult))
                st.add(tt(sinR, const("sinT"), rstd[:, :], ALU.mult))

                dve.wait_ge(*kv_ev(l, 5))
                heads = NAT[:, :, 0:192].rearrange("p t (h d) -> p t h d", h=3)
                x1, x2 = heads[:, :, :, 0:8], heads[:, :, :, 8:16]
                c, s = (const(n).rearrange("p (t i) -> p t i", t=5).unsqueeze(2).broadcast_to([P, 5, 3, 8])
                        for n in ("cosN", "sinN"))
                r4 = [TS[:, 120 * i:120 * i + 120].rearrange("p (t h i) -> p t h i", t=5, h=3) for i in range(4)]
                st.add(tt(r4[0], x1, c, ALU.mult))
                st.add(tt(r4[1], x2, s, ALU.mult))
                st.add(tt(r4[2], x2, c, ALU.mult))
                then_wait(tt(r4[3], x1, s, ALU.mult))
                tt(x1, r4[0], r4[1], ALU.subtract)
                tt(x2, r4[2], r4[3], ALU.add).then_inc(nat_ready.sem, 1)
                ts(WI[:, :, :], NAT[:, :, 192:200], 8 ** -0.5, None, ALU.mult).then_inc(nat_ready.sem, 1)
                dve.wait_ge(*nat_ready(l, 2))
                tt(wdiag[:, :, :], WI[0:8, 4, :].unsqueeze(1).broadcast_to([8, NB, 8]),
                   ident[0:8, 0:8].unsqueeze(2).broadcast_to([8, NB, 8]), ALU.mult).then_inc(wd_ready.sem, 1)

                def rope(j):
                    dst = qiT[:, j, :] if j < 4 else qT[:, j - 4, :]
                    if j:
                        dve.wait_ge(*rope_done(l, j))
                    if j < 4:
                        dve.wait_ge(*evac(l, QI_T + j + 1))
                        tt(QC[:, j % 2, :], QZ[:, j % 2, :], cosR, ALU.mult).then_inc(qc_ready.sem, 1)
                    dve.wait_ge(*rot_mm(l, j + 1))
                    tt(halves(TS[:, :]), ps[:, 6:8, 0:HT], halves(sinR), ALU.mult).then_inc(rot_used.sem, 1)
                    dve.wait_ge(*rot_used(l, j + 1))
                    dve.wait_ge(*qc_ready(l, j + 1))
                    tt(dst, TS[:, :], QC[:, j % 2, :], ALU.add).then_inc(rope_done.sem, 1)

                for j in range(4):
                    rope(j)

                def best(t, r):
                    lo, n = KEYS_BEFORE[t], P * (t + 1)
                    left = (SCT if r == 0 else WK)[:, lo:lo + n]
                    st.add(nc.vector.max(M8[:, t - 1, :], left))
                    return st.last()

                def taken(t, r):
                    lo, n = KEYS_BEFORE[t], P * (t + 1)
                    left = (SCT if r == 0 else WK)[:, lo:lo + n]
                    st.add(nc.vector.match_replace(WK[:, lo:lo + n], M8[:, t - 1, :], left, TAKEN))
                    return st.last()

                def chosen(t):
                    lo, n = KEYS_BEFORE[t], P * (t + 1)
                    tt(NOT[:, lo:lo + n], WK[:, lo:lo + n], SCT[:, lo:lo + n], ALU.is_ge
                       ).then_inc(sel_ready.sem, 1)

                found, left = {}, {}

                def find(t, r):
                    if r:
                        wait_alone(dve, *left[t])
                    found[t] = best(t, r)

                def take(t, r):
                    wait_alone(dve, *found[t])
                    left[t] = taken(t, r)

                def finish(t):
                    wait_alone(dve, *left[t])
                    chosen(t)

                for d in range(24):
                    t, h = 1 + d // 8, d % 8
                    n = P * (t + 1)
                    sc = SCT[:, KEYS_BEFORE[t]:KEYS_BEFORE[t] + n]
                    dve.wait_ge(*dot_relu(l, d + 1))
                    if h:
                        dve.wait_ge(*dot_acc(l, d))
                    stt(sc, RB[:, d % 4, 0:n], WI[:, t, h:h + 1],
                        sc if h else const("mask")[:, 384 - P * t:384 - P * t + n],
                        ALU.mult, ALU.add).then_inc(dot_acc.sem, 1)
                    if d == 7:
                        wait_alone(dve, *dot_acc(l, 8))
                    if d >= 8:
                        find(1, d - 8) if d == 8 else None
                        take(1, d - 8)
                        find(1, d - 7) if d < 23 else finish(1)
                wait_alone(dve, *dot_acc(l, 24))
                rounds = [(act_on, t, r) for r in range(TOPK_P // 8) for act_on in (find, take) for t in (2, 3)]
                rounds += [(finish, 2), (finish, 3)]
                for act_on, *at in rounds[:4 * EARLY_ROUNDS]:
                    act_on(*at)
                later = rounds[4 * EARLY_ROUNDS:]

                dve.wait_ge(*sdot_mm(l, 17))
                dve.wait_ge(*qib_ev(l, 5))
                for b in range(NB):
                    stt(SW[:, P * b:P * b + P].rearrange("p (j h) -> p j h", h=8),
                        ps[:, 6 + b // 4, P * (b % 4):P * (b % 4) + P].rearrange("p (j h) -> p j h", h=8), 0.0,
                        wbc[:, b:b + 1, :].broadcast_to([P, 16, 8]), ALU.max, ALU.mult).then_inc(sw_used.sem, 1)
                stt(sdot[:, :], ps[0:8, 4, 0:64], 0.0, wdiag[:, :, :].rearrange("p b h -> p (b h)"),
                    ALU.max, ALU.mult).then_inc(sw_used.sem, 1)
                dve.wait_ge(*sw_used(l, 9))
                nc.vector.tensor_reduce(sTok[:, :], SW.rearrange("p (c h) -> p c h", h=8), AX.X, ALU.add
                                        ).then_inc(stok_ready.sem, 1)
                nc.vector.tensor_reduce(snew[:, :], sdot[:, :], AX.X, ALU.add).then_inc(stok_ready.sem, 1)

                cand = candI[:, 0:1].bitcast(F32)
                thr = cols[:, 7:8]

                def count(s):
                    src, by = (S, 0.0) if s == 0 else (S2, cand)
                    ts(J[:, :], src[:, :], by, None, ALU.is_ge, ALU.add, accum_out=(cntB if s % 2 else cntA)
                       ).then_inc(cnt_ready.sem, 1)

                def counted(s):
                    return ps[0:64, 4 + s % 2, 300:301]

                def bits_start():
                    dve.wait_ge(*sT_ev(l, 1))
                    dve.wait_ge(*sT_mm(l, 2))
                    then_wait(tt(S[:, 256:257], ps[0:64, 5, 0:1], const("newneg", 64), ALU.add))
                    count(0)

                def bits_sign():
                    dve.wait_ge(*cnt_mm(l, 1))
                    then_wait(ts(cols[:, 8:9], counted(0), float(TOPK_S), -2.0, ALU.is_lt, ALU.mult))
                    st.add(ts(sgn, cols[:, 8:9], 1.0, None, ALU.add))
                    then_wait(ts(kth, cols[:, 8:9], -(PAST + 1 - 2 * TOPK_S + 1) / 2.0, float(TOPK_S),
                                 ALU.mult, ALU.add))
                    st.add(ts(S2[:, 0:256], S[:, 0:256], sgn, None, ALU.mult))
                    st.add(stt(S2[:, 256:257], ps[0:64, 5, 0:1], sgn, const("newneg", 64), ALU.mult, ALU.add))
                    then_wait(nc.vector.tensor_copy(candI[:, 0:1], const("bits", 64).bitcast(I32)[:, 30:31]))
                    count(1)

                def bit(s):
                    b = BITS - s
                    bits = const("bits", 64).bitcast(I32)
                    dve.wait_ge(*cnt_mm(l, s + 1))
                    then_wait(ts(candI[:, 1:2], counted(s), kth, float(1 << b), ALU.is_lt, ALU.mult))
                    if b:
                        then_wait(stt(candI[:, 0:1], candI[:, 1:2], bits[:, b - 1:b], candI[:, 0:1],
                                      ALU.bitwise_or, ALU.bitwise_xor))
                        count(s + 1)
                    else:
                        then_wait(tt(candI[:, 0:1], candI[:, 1:2], candI[:, 0:1], ALU.bitwise_xor))
                        then_wait(tt(thr, cand, sgn, ALU.mult))

                steps = [bits_start, bits_sign] + [lambda s=s: bit(s) for s in range(1, BITS + 1)]

                def pooled(g):
                    w = WINDOWS[g]
                    res = (LA[:, 0], LB[:, 0], LA[:, 2], LB[:, 2])[g]
                    edge = const("edge")[:, POOL_BUF * g:POOL_BUF * (g + 1)]
                    if g == 0:
                        dve.wait_ge(*sums_ready(l, 9))
                        dve.wait_ge(*evac(l, Q_T))
                    then_wait(tt(res[:, 15:30], res[:, 15:30], edge, ALU.mult))
                    stt(DIFF[:, g, 0:SEQ], res[:, 15:527], 1.0 / w, XPb[:, g, 15:527], ALU.mult, ALU.subtract
                        ).then_inc(diff_ready.sem, 1)
                    stt(DIFF[:, g, SEQ:TOK], XS[:, g, :], 1.0 / w - 1.0, prevs[:, 8 * g:8 * g + 8],
                        ALU.mult, ALU.add).then_inc(diff_ready.sem, 1)

                for pair in range(BITS // 2 + 1):
                    for _ in range(2):
                        steps.pop(0)()
                        left_steps = max(len(steps) - 1, 1)
                        for _ in range(-(-len(later) // left_steps)):
                            f, *a = later.pop(0)
                            f(*a)
                    for j in {8: (4,), 12: (5,), 15: (6, 7)}.get(pair, ()):
                        rope(j)
                    for g in {9: (0,), 10: (1,), 11: (2,), 13: (3,)}.get(pair, ()):
                        pooled(g)
                assert not later
                while steps:
                    steps.pop(0)()

                def pick_a():
                    ts(J[:, :], S[:, :], thr, None, ALU.is_gt, ALU.add, accum_out=cntA).then_inc(pick_ready.sem, 1)
                    ts(J2[:, :], S[:, :], thr, None, ALU.is_equal, ALU.add, accum_out=cntB
                       ).then_inc(pick_ready.sem, 1)

                def pick_b():
                    dve.wait_ge(*pick_mm(l, 2))
                    dve.wait_ge(*pick_ready(l, 2))
                    st.add(ts(need, ps[0:64, 3, 0:1], -1.0, float(TOPK_S), ALU.mult, ALU.add))
                    then_wait(nc.vector.tensor_copy(offs, ps[0:64, 3, 1:2]))
                    then_wait(nc.vector.tensor_tensor_scan(S2[:, :], J2[:, :], J2[:, :], offs, ALU.add, ALU.bypass))
                    then_wait(stt(S2[:, :], S2[:, :], need, J2[:, :], ALU.is_le, ALU.mult))
                    then_wait(tt(J[:, :], J[:, :], S2[:, :], ALU.add))
                    ts(J2[:, 0:256], J[:, 0:256], 1.0, None, ALU.mult, ALU.add, accum_out=cntA
                       ).then_inc(pick_ready.sem, 1)

                def pick_c():
                    dve.wait_ge(*pick_mm(l, 4))
                    st.add(nc.vector.tensor_copy(snegc, ps[0:64, 3, 3:4]))
                    then_wait(nc.vector.tensor_copy(offs, ps[0:64, 3, 2:3]))
                    then_wait(nc.vector.tensor_tensor_scan(S2[:, 0:256], J[:, 0:256], J[:, 0:256], offs,
                                                           ALU.add, ALU.bypass))
                    tt(S2[:, 0:256], S2[:, 0:256], J[:, 0:256], ALU.mult).then_inc(pick_ready.sem, 1)

                def pick_d():
                    dve.wait_ge(*pos_mm(l, 1))
                    then_wait(ts(posI[:, 0, :], ps[:, 3, P:2 * P], -1.0, None, ALU.add))
                    st.add(ts(posI[:, 1, :], posI[:, 0, :], 4, None, ALU.arith_shift_right))
                    then_wait(ts(posI[:, 2, :], posI[:, 0, :], 15, None, ALU.bitwise_and))
                    iota = const("iota16").unsqueeze(1).broadcast_to([P, P, 16])

                    def wide(ap):
                        return ap.unsqueeze(2).broadcast_to([P, P, 16])
                    st.add(tt(OA[:, :, :], wide(posI[:, 1, :]), iota, ALU.is_equal))
                    then_wait(tt(OB[:, :, 1, :], wide(posI[:, 2, :]), iota, ALU.is_equal))
                    then_wait(tt(OB[:, :, 0, :], OB[:, :, 1, :], wide(phys[:, :, :, :].rearrange("p g b j -> p (g b j)")),
                                 ALU.mult))
                    ts(OB[:, :, 1, :], OB[:, :, 1, :], const("tok"), None, ALU.mult).then_inc(hot_ready.sem, 1)

                def pick_e():
                    dve.wait_ge(*list_ev(l, 1))
                    then_wait(stt(ixf[:, :, :], ix[:, 0], float(PAGE), ix[:, 1], ALU.mult, ALU.add))
                    ts(ixi[:, :, :], ixf[:, :, :], base[0:16, :], None, ALU.add).then_inc(list_ready.sem, 1)

                picks = {0: pick_a, 2: pick_b, 4: pick_c, 6: pick_d, 14: pick_e}

                def masked(i):
                    t = i // N_HEADS
                    n = P * (t + 1)
                    dve.wait_ge(*qk_mm(l, i + 1))
                    if i >= 2:
                        dve.wait_ge(*exp_done(l, i - 1))
                    if t == 0:
                        tt(ARS[:, i % 2, 0:n], ps[:, i % 3, 0:n], const("mask")[:, 384:512], ALU.add
                           ).then_inc(qk_used.sem, 1)
                    else:
                        stt(ARS[:, i % 2, 0:n], NOT[:, KEYS_BEFORE[t]:KEYS_BEFORE[t] + n], NEG, ps[:, i % 3, 0:n],
                            ALU.mult, ALU.add).then_inc(qk_used.sem, 1)
                    dve.wait_ge(*qk_used(l, i + 1))
                    nc.vector.tensor_reduce(att[:, i % 4, 0:1], ARS[:, i % 2, 0:n], AX.X, ALU.max, negate=True
                                            ).then_inc(neg_max.sem, 1)

                def normalised(i):
                    n = P * (1 + i // N_HEADS)
                    dve.wait_ge(*exp_done(l, i + 1))
                    then_wait(nc.vector.reciprocal(att[:, i % 4, 2:3], att[:, i % 4, 1:2]))
                    ts(ARP[:, i % 4, 0:n], ARP[:, i % 4, 0:n], att[:, i % 4, 2:3], None, ALU.mult
                       ).then_inc(prob_ready.sem, 1)

                dve.wait_ge(*sel_ready(l, 3))
                for i in range(UNITS + 1):
                    if i < UNITS:
                        masked(i)
                    if i in picks:
                        picks[i]()
                    if i >= 1:
                        normalised(i - 1)

                dve.wait_ge(*qs_mm(l, 3))
                dve.wait_ge(*qs_ev(l, 2))
                then_wait(tt(tmp8[:, :], ps[0:64, 3, 400:408], const("diag", 64), ALU.mult))
                then_wait(nc.vector.tensor_reduce(SA[:, 256:257], tmp8[:, :], AX.X, ALU.add))
                then_wait(ts(cols[:, 9:10], snegc, -NEG, NEG, ALU.mult, ALU.add))
                st.add(tt(SA[:, 256:257], SA[:, 256:257], cols[:, 9:10], ALU.add))
                then_wait(stt(SA[:, 255:256], snegc, NEG, SA[:, 255:256], ALU.mult, ALU.add))
                nc.vector.tensor_reduce(sm[:, 0:1], SA[:, :], AX.X, ALU.max, negate=True).then_inc(ss_ready.sem, 1)
                dve.wait_ge(*se_ready(l, 1))
                then_wait(nc.vector.reciprocal(sm[:, 2:3], sm[:, 1:2]))
                ts(PA[:, :], PA[:, :], sm[:, 2:3], None, ALU.mult).then_inc(sp_ready.sem, 1)
                dve.wait_ge(*sp_ready(l, 1))
                ts(pnd[:, :], const("diag", 64), PA[:, 256:257], None, ALU.mult).then_inc(sp_ready.sem, 1)
                st.add(ts(base[:, :], base[:, :], float(N_PHYS * PAGE), None, ALU.add))

                def lower_out(c):
                    dve.wait_ge(*ohi_ready(l, c + 1))
                    tt(lower_w(c % 2, 0, 2048), wslot(c)[:, 0:2048], OH[c % 2], ALU.subtract
                       ).then_inc(olo_ready.sem, 1)

                def lower_mixed(tiles):
                    for k in tiles:
                        dve.wait_ge(*mhi_ready(l, k + 1))
                        k = MIX_ORDER[k]
                        tt(tile_of("hT", k), hT[:, k, :], MH[k], ALU.subtract).then_inc(mlo_ready.sem, 1)
                lower_mixed(range(4))
                lower_out(0)
                lower_mixed(range(4, KD))
                lower_out(1)

                def lower_weights(i, u, a):
                    dve.wait_ge(*whi_ready(l, i * 2 + (a + 1)))
                    at = slice(1024 * a, 1024 * (a + 1))
                    tt(lower_w(u, at.start, at.stop), W[:, u, at], WH[u][:, at], ALU.subtract
                       ).then_inc(wlo_ready.sem, 1)

                def lower_down(m):
                    for p, part in enumerate(DH[m % 2]):
                        dve.wait_ge(*whi_ready(l, 2 * NF + 2 * m + p + 1))
                        for k0, at, n in part:
                            last = tt(lower_w(m % 2, P * k0, P * (k0 + n)), wslot(m)[:, P * k0:P * (k0 + n)], at,
                                      ALU.subtract)
                        last.then_inc(wlo_ready.sem, 1)

                def lower_y(tiles):
                    for k in tiles:
                        dve.wait_ge(*yhi_ready(l, k + 1))
                        tt(tile_of("yR", k), yT[:, k, :], YH[k], ALU.subtract).then_inc(ylo_ready.sem, 1)

                def lower_h(k):
                    dve.wait_ge(*hhi_ready(l, k + 1))
                    stt(tile_of("hT", k), xT[:, k, :], gain(G_PRE_FFN, k), tile_of("moR", k), ALU.mult,
                        ALU.subtract).then_inc(hlo_ready.sem, 1)

                def before_add(k):
                    if k in (2, 4):
                        lower_out(k // 2 + 1)
                    if k == KD - 1:
                        for a in range(2):
                            lower_weights(0, 0, a)
                update(l, 1, G_POST_MIX, lambda k: evac(l, WO_T + k + 1), before_add,
                       lambda k: lower_h(k - 2) if k >= 2 else None)
                lower_h(KD - 2)
                lower_h(KD - 1)
                sum_squares(l, 2, lambda k: sq_ready(l, KD + k + 1))
                for a in range(2):
                    lower_weights(1, 1, a)
                inverse_root(l, 2)

                for u in range(2):
                    ms = nc.vector.memset(G[:, u, 0:2], 0.0)
                then_wait(ms)
                st.end()

                def conv_tile(i, u, rnd, first, split_next=True):
                    fs = ffn_step
                    fs.begin(rnd * 2 + u)
                    col = (lambda at: V[:, at + i:at + i + 1]) if isinstance(i, int) else \
                        (lambda at: V[:, bass.ds(i + at, 1)])
                    w0, w1, w2, bias = (col(a) for a in (36, 36 + NF, 36 + 2 * NF, 102))
                    cs = conv_T[:, i:i + 1, :] if isinstance(i, int) else conv_T[:, bass.ds(i, 1), :]
                    cs = cs.rearrange("p a (b j) -> p (a b) j", j=2)
                    g, cv = G[:, u, :], CV[:, u, :]
                    if split_next:
                        lower_weights(i + 1, 1 - u, 0)
                    dve.wait_ge(*tile_done(l, i * 2 + (GV_T + 1)))
                    if first:
                        dve.wait_ge(*rstd_ready(l, 2))
                    else:
                        dve.wait_ge(*conv_done(l, i - 1))
                        dve.wait_ge(*co_mm(l, i - 1))
                    tt(halves(G[:, u, 2:522]), main(0), halves(rstd[:, :]), ALU.mult).then_inc(gate_ev.sem, 1)
                    dve.wait_ge(*gate_ev(l, i + 1))
                    if not first:
                        dve.wait_ge(*gelu_done(l, i - 1))
                    fs.add(ts(cv[:, 0:SEQ], g[:, 0:SEQ], w0, bias, ALU.mult, ALU.add))
                    fs.add(ts(cv[:, SEQ:TOK], cs[:, :, 0], w0, bias, ALU.mult, ALU.add))
                    dve.wait_ge(*fs.last())
                    fs.add(stt(cv[:, 0:SEQ], g[:, 1:SEQ + 1], w1, cv[:, 0:SEQ], ALU.mult, ALU.add))
                    fs.add(stt(cv[:, SEQ:TOK], cs[:, :, 1], w1, cv[:, SEQ:TOK], ALU.mult, ALU.add))
                    dve.wait_ge(*fs.last())
                    stt(cv[:, :], g[:, 2:TOK + 2], w2, cv[:, :], ALU.mult, ALU.add).then_inc(conv_done.sem, 1)
                    if split_next:
                        lower_weights(i + 1, 1 - u, 1)
                    dve.wait_ge(*gelu_done(l, i + 1))
                    fs.add(tt(GE[:, u, :], GE[:, u, :], rstd[:, :], ALU.mult))
                    dve.wait_ge(*fs.last())
                    fs.end()
                    dve.wait_ge(*tile_done(l, i * 2 + (GV_T + 2)))
                    y = yT[:, i:i + 1, :] if isinstance(i, int) else yT[:, bass.ds(i, 1), :]
                    tt(y.rearrange("p a (f t) -> p (a f) t", f=2), halves(GE[:, u, :]), main(1), ALU.mult
                       ).then_inc(val_used.sem, 1)

                conv_tile(0, 0, l * (NF // 2), True, False)
                conv_tile(1, 1, l * (NF // 2), True)
                with dve.Fori(1, NF // 2 - 1) as r:
                    for u in range(2):
                        conv_tile(r * 2 + u, u, l * (NF // 2) + r, False)
                last = l * (NF // 2) + (NF // 2 - 1)
                conv_tile(NF - 2, 0, last, False)
                lower_y(range(6))
                conv_tile(NF - 1, 1, last, False, False)
                lower_down(0)
                lower_y(range(6, NF))
                lower_down(1)
                update(l, 3, G_POST_FFN, lambda k: evac(l, EVAC_DN + k + 1),
                       lambda k: lower_down(k + 1) if k + 1 < KD else None)

            with dve.Fori(0, DEPTH) as l:
                layer(l)


_SHAPES = {
    "y_prompt": (1, SEQ, D_MODEL), "y_sample": (NB, 1, D_MODEL),
    "new_k_prompt": (DEPTH, 1, SEQ, 2, HD), "new_v_prompt": (DEPTH, 1, SEQ, 2, HD),
    "new_ik_prompt": (DEPTH, 1, SEQ, HD), "new_pool_prompt": (DEPTH, 1, POOL_BUF, 512),
    "new_conv_prompt": (DEPTH, 1, 2, D_FF),
    "new_k_sample": (DEPTH, NB, 1, 2, HD), "new_v_sample": (DEPTH, NB, 1, 2, HD),
    "new_ik_sample": (DEPTH, NB, 1, HD), "new_pool_sample": (DEPTH, NB, POOL_BUF, 512),
    "new_conv_sample": (DEPTH, NB, 2, D_FF),
}


def kernel(**inputs):
    import concourse.bacc as bacc
    from concourse.bass_utils import run_bass_kernel_spmd

    nc = bacc.Bacc("TRN2", target_bir_lowering=False, num_devices=1)
    arrays = {f"in_{n}": np.ascontiguousarray(a) for n, a in inputs.items()}
    arrays["in_consts"] = constants()
    A = {n[3:]: nc.dram_tensor(n, a.shape, mybir.dt.from_np(a.dtype), kind="ExternalInput").ap()
         for n, a in arrays.items()}
    O = {n: nc.dram_tensor(f"out_{n}", s, F32, kind="ExternalOutput").ap() for n, s in _SHAPES.items()}
    scratch = nc.dram_tensor("slot_lists", (NB, TOPK_S), I32, kind="Internal").ap()
    build(nc, A, O, scratch)
    r = run_bass_kernel_spmd(nc, [arrays], core_ids=[0])
    return tuple(r.results[0][f"out_{n}"] for n in _SHAPES)
```
